# Optimizing a Trainium2 kernel written in Bass

```python
import math
import jax, jax.numpy as jnp
from jax import lax
import numpy as np

D_MODEL = 1024
BATCH = 1
SEQ = 256
DEPTH = 2

MEM_LEN = 256
EPS = 1e-6
D_FF = 2816
CONV_WIDTH = 3
CONV_CH = D_MODEL // 2
SWA_HEADS = 8
SWA_KV_HEADS = 2
SWA_HEAD_DIM = 64
WINDOW = 128
MOBA_HEADS = 8
MOBA_KV_HEADS = 4
MOBA_HEAD_DIM = D_MODEL // MOBA_HEADS
MOBA_BLOCK = 256
MOBA_TOPK = 3
MOBA_Q_CHUNK = 16
REL_BUCKETS = 32
REL_MAX_DIST = 128
REL_HEADS = SWA_HEADS
XA_HEADS = 4
XA_HEAD_DIM = 128
XA_W = XA_HEADS * XA_HEAD_DIM

N_EVEN = (DEPTH + 1) // 2
N_ODD = DEPTH // 2
SWA_Q_W = SWA_HEADS * SWA_HEAD_DIM
SWA_KV_W = SWA_KV_HEADS * SWA_HEAD_DIM
EVEN_IN = 3 * CONV_CH + SWA_Q_W + 2 * SWA_KV_W
EVEN_MIX = CONV_CH + SWA_Q_W
MOBA_Q_W = MOBA_HEADS * MOBA_HEAD_DIM
MOBA_KV_W = MOBA_KV_HEADS * MOBA_HEAD_DIM
ODD_IN = MOBA_Q_W + 2 * MOBA_KV_W


def rmsnorm(x, g):
    x32 = x.astype(jnp.float32)
    y = x32 * lax.rsqrt(jnp.mean(x32 * x32, axis=-1, keepdims=True) + EPS)
    return y.astype(x.dtype) * g

def swiglu(x, w_gate, w_up, w_down):
    return (jax.nn.silu(x @ w_gate) * (x @ w_up)) @ w_down

def rel_bucket(dist):
    n = jnp.maximum(dist, 0)
    max_exact = REL_BUCKETS // 2
    nf = jnp.maximum(n, 1).astype(jnp.float32)
    large = max_exact + (jnp.log(nf / max_exact) / math.log(REL_MAX_DIST / max_exact)
                         * (REL_BUCKETS - max_exact)).astype(jnp.int32)
    large = jnp.minimum(large, REL_BUCKETS - 1)
    return jnp.where(n < max_exact, n, large)

def short_conv_mixer(b_gate, c_gate, u, conv_w):
    v = c_gate * u
    S = v.shape[1]
    vp = jnp.pad(v, ((0, 0), (CONV_WIDTH - 1, 0), (0, 0)))
    conv = vp[:, 0:S] * conv_w[0]
    for j in range(1, CONV_WIDTH):
        conv = conv + vp[:, j:j + S] * conv_w[j]
    return b_gate * conv

def sliding_window_attention(q, k, v, sinks, table):
    B, S, H, dh = q.shape
    Hkv = k.shape[2]
    G = H // Hkv
    nb = S // WINDOW
    qb = q.reshape(B, nb, WINDOW, Hkv, G, dh)

    def with_prev(t):
        t = t.reshape(B, nb, WINDOW, Hkv, dh)
        prev = jnp.pad(t, ((0, 0), (1, 0), (0, 0), (0, 0), (0, 0)))[:, :-1]
        return jnp.concatenate([prev, t], axis=2)

    kc, vc = with_prev(k), with_prev(v)
    logits = jnp.einsum('bnqkgd,bnjkd->bnkgqj', qb, kc).astype(jnp.float32) * dh ** -0.5
    qi = jnp.arange(WINDOW)[:, None]
    kj = jnp.arange(2 * WINDOW)[None, :]
    dist = qi + WINDOW - kj
    band = (dist >= 0) & (dist < WINDOW)
    mask = band[None] & ((jnp.arange(nb)[:, None, None] > 0) | (kj >= WINDOW)[None])
    bias = jnp.moveaxis(table[rel_bucket(dist)], -1, 0).reshape(Hkv, G, WINDOW, 2 * WINDOW)
    logits = jnp.where(mask[None, :, None, None], logits + bias, -jnp.inf)
    sink = sinks.astype(jnp.float32).reshape(Hkv, G)[None, None, :, :, None, None]
    m = jnp.maximum(jnp.max(logits, axis=-1, keepdims=True), sink)
    p = jnp.exp(logits - m)
    p = p / (jnp.sum(p, axis=-1, keepdims=True) + jnp.exp(sink - m))
    out = jnp.einsum('bnkgqj,bnjkd->bnqkgd', p.astype(v.dtype), vc)
    return out.reshape(B, S, H * dh)

def moba_attention(q, k, v, table):
    B, S, H, dh = q.shape
    Hkv = k.shape[2]
    G = H // Hkv
    s_pad = -(-S // MOBA_BLOCK) * MOBA_BLOCK
    nblk = s_pad // MOBA_BLOCK
    pad = ((0, 0), (0, s_pad - S), (0, 0), (0, 0))
    kblk = jnp.pad(k, pad).reshape(B, nblk, MOBA_BLOCK, Hkv, dh).transpose(0, 3, 1, 2, 4)
    vblk = jnp.pad(v, pad).reshape(B, nblk, MOBA_BLOCK, Hkv, dh).transpose(0, 3, 1, 2, 4)
    kmean = jnp.mean(kblk.astype(jnp.float32), axis=3)
    nq = S // MOBA_Q_CHUNK
    qc = q.reshape(B, nq, MOBA_Q_CHUNK, Hkv, G, dh).transpose(1, 0, 3, 4, 2, 5)
    topk = min(MOBA_TOPK, nblk)
    n_sel = topk * MOBA_BLOCK
    scale = dh ** -0.5
    b_ix = jnp.arange(B)[:, None, None, None, None]
    k_ix = jnp.arange(Hkv)[None, :, None, None, None]
    tbl = table.T.reshape(Hkv, G, REL_BUCKETS)
    k6 = jnp.arange(Hkv)[None, :, None, None, None, None]
    g6 = jnp.arange(G)[None, None, :, None, None, None]
    blk_ids = jnp.arange(nblk)
    offs = jnp.arange(MOBA_BLOCK)

    def one_chunk(args):
        ci, qx = args
        t = ci * MOBA_Q_CHUNK + jnp.arange(MOBA_Q_CHUNK)
        own = (ci * MOBA_Q_CHUNK) // MOBA_BLOCK
        gate = jnp.einsum('bkgqd,bknd->bkgqn', qx.astype(jnp.float32), kmean)
        gate = jnp.where(blk_ids < own, gate, -jnp.inf)
        _, sel = lax.top_k(gate, topk)
        valid = sel < own
        ks = kblk[b_ix, k_ix, sel]
        vs = vblk[b_ix, k_ix, sel]
        dist_sel = t[:, None, None] - (sel[..., None] * MOBA_BLOCK + offs)
        l_sel = jnp.einsum('bkgqd,bkgqsnd->bkgqsn', qx, ks).astype(jnp.float32) * scale
        l_sel = jnp.where(valid[..., None], l_sel + tbl[k6, g6, rel_bucket(dist_sel)], -jnp.inf)
        k_own = lax.dynamic_index_in_dim(kblk, own, axis=2, keepdims=False)
        v_own = lax.dynamic_index_in_dim(vblk, own, axis=2, keepdims=False)
        dist_own = t[:, None] - (own * MOBA_BLOCK + offs)[None, :]
        l_own = jnp.einsum('bkgqd,bknd->bkgqn', qx, k_own).astype(jnp.float32) * scale
        l_own = jnp.where(dist_own >= 0, l_own + tbl[:, :, rel_bucket(dist_own)], -jnp.inf)
        logits = jnp.concatenate([l_sel.reshape(l_sel.shape[:4] + (n_sel,)), l_own], axis=-1)
        p = jax.nn.softmax(logits, axis=-1).astype(v.dtype)
        p_sel = p[..., :n_sel].reshape(l_sel.shape)
        return (jnp.einsum('bkgqsn,bkgqsnd->bkgqd', p_sel, vs)
                + jnp.einsum('bkgqn,bknd->bkgqd', p[..., n_sel:], v_own))

    out = lax.map(one_chunk, (jnp.arange(nq), qc))
    return out.transpose(1, 0, 4, 2, 3, 5).reshape(B, S, H * dh)

def even_mixer(h, w_in, conv_w, sinks, w_out, table):
    B, S, _ = h.shape
    z = h @ w_in
    c1 = CONV_CH
    c2 = 2 * CONV_CH
    c3 = 3 * CONV_CH
    c4 = c3 + SWA_Q_W
    c5 = c4 + SWA_KV_W
    b_gate, c_gate, u, q, k, v = jnp.split(z, [c1, c2, c3, c4, c5], axis=-1)
    ya = short_conv_mixer(b_gate, c_gate, u, conv_w)
    yb = sliding_window_attention(q.reshape(B, S, SWA_HEADS, SWA_HEAD_DIM),
                                  k.reshape(B, S, SWA_KV_HEADS, SWA_HEAD_DIM),
                                  v.reshape(B, S, SWA_KV_HEADS, SWA_HEAD_DIM), sinks, table)
    return jnp.concatenate([ya, yb], axis=-1) @ w_out

def odd_mixer(h, w_in, w_out, table):
    B, S, _ = h.shape
    z = h @ w_in
    q, k, v = jnp.split(z, [MOBA_Q_W, MOBA_Q_W + MOBA_KV_W], axis=-1)
    y = moba_attention(q.reshape(B, S, MOBA_HEADS, MOBA_HEAD_DIM),
                       k.reshape(B, S, MOBA_KV_HEADS, MOBA_HEAD_DIM),
                       v.reshape(B, S, MOBA_KV_HEADS, MOBA_HEAD_DIM), table)
    return y @ w_out

def memory_cross_attention(h, mem_n, w_q, w_kv, w_o):
    B, S, _ = h.shape
    M = mem_n.shape[1]
    q = (h @ w_q).reshape(B, S, XA_HEADS, XA_HEAD_DIM)
    kv = (mem_n @ w_kv).reshape(B, M, 2, XA_HEADS, XA_HEAD_DIM)
    k, v = kv[:, :, 0], kv[:, :, 1]
    logits = jnp.einsum('bshd,bmhd->bhsm', q, k).astype(jnp.float32) * XA_HEAD_DIM ** -0.5
    p = jax.nn.softmax(logits, axis=-1).astype(v.dtype)
    o = jnp.einsum('bhsm,bmhd->bshd', p, v).reshape(B, S, XA_W)
    return o @ w_o

def first_inputs(seed: int = 0) -> dict:
    key = jax.random.key(seed)
    ks = jax.random.split(key, 32)
    f32 = jnp.float32

    def w(k, shape, fan_in):
        return jax.random.normal(k, shape, f32) * fan_in ** -0.5

    def gain(k, shape):
        return 1.0 + 0.02 * jax.random.normal(k, shape, f32)

    return {
        'x': jax.random.normal(ks[0], (BATCH, SEQ, D_MODEL), f32),
        'mem': jax.random.normal(ks[1], (BATCH, MEM_LEN, D_MODEL), f32),
        'ffn1_norm': gain(ks[2], (DEPTH, D_MODEL)),
        'ffn1_w_gate': w(ks[3], (DEPTH, D_MODEL, D_FF), D_MODEL),
        'ffn1_w_up': w(ks[4], (DEPTH, D_MODEL, D_FF), D_MODEL),
        'ffn1_w_down': w(ks[5], (DEPTH, D_FF, D_MODEL), D_FF),
        'mix_norm': gain(ks[6], (DEPTH, D_MODEL)),
        'ev_w_in': w(ks[7], (N_EVEN, D_MODEL, EVEN_IN), D_MODEL),
        'ev_conv_w': w(ks[8], (N_EVEN, CONV_WIDTH, CONV_CH), CONV_WIDTH),
        'ev_sinks': 0.5 * jax.random.normal(ks[9], (N_EVEN, SWA_HEADS), f32),
        'ev_w_out': w(ks[10], (N_EVEN, EVEN_MIX, D_MODEL), EVEN_MIX),
        'od_w_in': w(ks[11], (N_ODD, D_MODEL, ODD_IN), D_MODEL),
        'od_w_out': w(ks[12], (N_ODD, MOBA_Q_W, D_MODEL), MOBA_Q_W),
        'rel_bias': 0.2 * jax.random.normal(ks[13], (REL_BUCKETS, REL_HEADS), f32),
        'xa_norm': gain(ks[14], (DEPTH, D_MODEL)),
        'xa_w_q': w(ks[15], (DEPTH, D_MODEL, XA_W), D_MODEL),
        'xa_w_kv': w(ks[16], (DEPTH, D_MODEL, 2 * XA_W), D_MODEL),
        'xa_w_o': w(ks[17], (DEPTH, XA_W, D_MODEL), XA_W),
        'mem_norm': gain(ks[18], (D_MODEL,)),
        'ffn2_norm': gain(ks[19], (DEPTH, D_MODEL)),
        'ffn2_w_gate': w(ks[20], (DEPTH, D_MODEL, D_FF), D_MODEL),
        'ffn2_w_up': w(ks[21], (DEPTH, D_MODEL, D_FF), D_MODEL),
        'ffn2_w_down': w(ks[22], (DEPTH, D_FF, D_MODEL), D_FF),
        'final_norm': gain(ks[23], (D_MODEL,)),
    }

def first_block(x, mem, ffn1_norm, ffn1_w_gate, ffn1_w_up, ffn1_w_down, mix_norm,
              ev_w_in, ev_conv_w, ev_sinks, ev_w_out, od_w_in, od_w_out, rel_bias,
              xa_norm, xa_w_q, xa_w_kv, xa_w_o, mem_norm,
              ffn2_norm, ffn2_w_gate, ffn2_w_up, ffn2_w_down, final_norm):
    mem_n = rmsnorm(mem, mem_norm)
    for l in range(DEPTH):
        x = x + 0.5 * swiglu(rmsnorm(x, ffn1_norm[l]), ffn1_w_gate[l], ffn1_w_up[l], ffn1_w_down[l])
        h = rmsnorm(x, mix_norm[l])
        if l % 2 == 0:
            i = l // 2
            x = x + even_mixer(h, ev_w_in[i], ev_conv_w[i], ev_sinks[i], ev_w_out[i], rel_bias)
        else:
            i = l // 2
            x = x + odd_mixer(h, od_w_in[i], od_w_out[i], rel_bias)
        x = x + memory_cross_attention(rmsnorm(x, xa_norm[l]), mem_n, xa_w_q[l], xa_w_kv[l], xa_w_o[l])
        x = x + 0.5 * swiglu(rmsnorm(x, ffn2_norm[l]), ffn2_w_gate[l], ffn2_w_up[l], ffn2_w_down[l])
    return rmsnorm(x, final_norm)


DEPTH_2 = 1

CHUNK = 64
D_PLE = 256
D_CONV = 512
CONV_WIDTH_2 = 31
N_HEADS_GLA = 4
D_GLA_K = 256
D_GLA_V = 512
HEAD_K = D_GLA_K // N_HEADS_GLA
HEAD_V = D_GLA_V // N_HEADS_GLA
GATE_RANK = 16
GATE_TAU = 16.0
D_MIX = D_CONV + D_GLA_V
D_IN = 2 * D_CONV + 2 * D_GLA_K + 2 * D_GLA_V + GATE_RANK
SPLIT_POINTS = (
    D_CONV,
    2 * D_CONV,
    2 * D_CONV + D_GLA_K,
    2 * D_CONV + 2 * D_GLA_K,
    2 * D_CONV + 2 * D_GLA_K + D_GLA_V,
    2 * D_CONV + 2 * D_GLA_K + 2 * D_GLA_V,
)


def _rmsnorm(x, g):
    xf = x.astype(jnp.float32)
    y = xf * lax.rsqrt(jnp.mean(xf * xf, axis=-1, keepdims=True) + EPS)
    return (y * g.astype(jnp.float32)).astype(x.dtype)

def _layernorm(x, g, b):
    xf = x.astype(jnp.float32)
    mu = jnp.mean(xf, axis=-1, keepdims=True)
    var = jnp.mean(jnp.square(xf - mu), axis=-1, keepdims=True)
    y = (xf - mu) * lax.rsqrt(var + EPS)
    return (y * g.astype(jnp.float32) + b.astype(jnp.float32)).astype(x.dtype)

def _swiglu(x, w_in, w_out):
    gate, up = jnp.split(x @ w_in, 2, axis=-1)
    return (jax.nn.silu(gate) * up) @ w_out

def _conv_module(a, b, w_dw, b_dw, ln_g, ln_b):
    glu = a * jax.nn.sigmoid(b)
    y = lax.conv_general_dilated(
        glu, w_dw[:, None, :],
        window_strides=(1,),
        padding=((CONV_WIDTH_2 - 1, 0),),
        dimension_numbers=("NWC", "WIO", "NWC"),
        feature_group_count=D_CONV,
    ) + b_dw
    return jax.nn.silu(_layernorm(y, ln_g, ln_b))

def _to_chunks(t, n_heads):
    bsz, seq, width = t.shape
    return t.reshape(bsz, seq // CHUNK, CHUNK, n_heads, width // n_heads).transpose(0, 1, 3, 2, 4)

def _gla(q, k, v, r, g_lr, w_gate_up, b_gate, o_norm):
    bsz, seq, _ = q.shape
    f32 = jnp.float32
    log_a = jax.nn.log_sigmoid((g_lr @ w_gate_up + b_gate).astype(f32)) / GATE_TAU
    qc = _to_chunks(q.astype(f32), N_HEADS_GLA) * (HEAD_K ** -0.5)
    kc = _to_chunks(k.astype(f32), N_HEADS_GLA)
    vc = _to_chunks(v.astype(f32), N_HEADS_GLA)
    cum = jnp.cumsum(_to_chunks(log_a, N_HEADS_GLA), axis=3)
    e_pos = jnp.exp(cum)
    e_neg = jnp.exp(-cum)
    q_dec = qc * e_pos
    a_low = jnp.einsum("bnhtd,bnhsd->bnhts", q_dec, kc * e_neg)
    a_up = jnp.einsum("bnhtd,bnhsd->bnhts", qc * e_neg, kc * e_pos)
    pos = jnp.arange(CHUNK)
    scores = jnp.where(pos[:, None] >= pos[None, :], a_low, a_up)
    o_intra = jnp.einsum("bnhts,bnhsv->bnhtv", scores, vc)
    cum_end = cum[:, :, :, -1:, :]
    kv = jnp.einsum("bnhsd,bnhsv->bnhdv", kc * jnp.exp(cum_end - cum), vc)
    decay = jnp.exp(cum_end[:, :, :, 0, :])

    def step(state, inp):
        dec, kv_c = inp
        return dec[..., None] * state + kv_c, state

    s0 = jnp.zeros((bsz, N_HEADS_GLA, HEAD_K, HEAD_V), f32)
    _, s_prev = lax.scan(step, s0, (jnp.moveaxis(decay, 1, 0), jnp.moveaxis(kv, 1, 0)))
    s_prev = jnp.moveaxis(s_prev, 0, 1)
    o_inter = jnp.einsum("bnhtd,bnhdv->bnhtv", q_dec, s_prev)
    o = (o_intra + o_inter).transpose(0, 1, 3, 2, 4).reshape(bsz, seq, N_HEADS_GLA, HEAD_V)
    o = o * lax.rsqrt(jnp.mean(o * o, axis=-1, keepdims=True) + EPS)
    o = o * o_norm.astype(f32).reshape(N_HEADS_GLA, HEAD_V)
    return (o.reshape(bsz, seq, D_GLA_V) * jax.nn.silu(r.astype(f32))).astype(q.dtype)

def second_inputs(seed: int = 0) -> dict:
    key = jax.random.key(seed)
    ks = jax.random.split(key, 24)
    f32 = jnp.float32

    def w(k, shape, fan_in):
        return jax.random.normal(k, shape, f32) * (fan_in ** -0.5)

    def gain(k, shape):
        return 1.0 + 0.05 * jax.random.normal(k, shape, f32)

    def bias(k, shape, scale=0.02):
        return scale * jax.random.normal(k, shape, f32)

    return {
        "x": jax.random.normal(ks[0], (BATCH, SEQ, D_MODEL), f32),
        "p": jax.random.normal(ks[1], (DEPTH_2, BATCH, SEQ, D_PLE), f32),
        "ffn1_norm": gain(ks[2], (DEPTH_2, D_MODEL)),
        "ffn1_w_in": w(ks[3], (DEPTH_2, D_MODEL, 2 * D_FF), D_MODEL),
        "ffn1_w_out": w(ks[4], (DEPTH_2, D_FF, D_MODEL), D_FF),
        "mix_norm": gain(ks[5], (DEPTH_2, D_MODEL)),
        "w_in": w(ks[6], (DEPTH_2, D_MODEL, D_IN), D_MODEL),
        "conv_w": w(ks[7], (DEPTH_2, CONV_WIDTH_2, D_CONV), CONV_WIDTH_2),
        "conv_b": bias(ks[8], (DEPTH_2, D_CONV)),
        "conv_ln_g": gain(ks[9], (DEPTH_2, D_CONV)),
        "conv_ln_b": bias(ks[10], (DEPTH_2, D_CONV)),
        "gate_w_up": w(ks[11], (DEPTH_2, GATE_RANK, D_GLA_K), GATE_RANK),
        "gate_b": bias(ks[12], (DEPTH_2, D_GLA_K), 0.1),
        "gla_norm": gain(ks[13], (DEPTH_2, D_GLA_V)),
        "w_out": w(ks[14], (DEPTH_2, D_MIX, D_MODEL), D_MIX),
        "ffn2_norm": gain(ks[15], (DEPTH_2, D_MODEL)),
        "ffn2_w_in": w(ks[16], (DEPTH_2, D_MODEL, 2 * D_FF), D_MODEL),
        "ffn2_w_out": w(ks[17], (DEPTH_2, D_FF, D_MODEL), D_FF),
        "ple_norm": gain(ks[18], (DEPTH_2, D_MODEL)),
        "ple_w_gate": w(ks[19], (DEPTH_2, D_MODEL, D_MODEL), D_MODEL),
        "ple_w_proj": w(ks[20], (DEPTH_2, D_PLE, D_MODEL), D_PLE),
        "final_norm": gain(ks[21], (D_MODEL,)),
    }

def second_block(x, p, ffn1_norm, ffn1_w_in, ffn1_w_out, mix_norm, w_in, conv_w, conv_b,
              conv_ln_g, conv_ln_b, gate_w_up, gate_b, gla_norm, w_out, ffn2_norm,
              ffn2_w_in, ffn2_w_out, ple_norm, ple_w_gate, ple_w_proj, final_norm):
    h = x
    for i in range(DEPTH_2):
        h = h + 0.5 * _swiglu(_rmsnorm(h, ffn1_norm[i]), ffn1_w_in[i], ffn1_w_out[i])
        z = _rmsnorm(h, mix_norm[i]) @ w_in[i]
        conv_a, conv_gt, q, k, v, r, g_lr = jnp.split(z, SPLIT_POINTS, axis=-1)
        y_conv = _conv_module(conv_a, conv_gt, conv_w[i], conv_b[i], conv_ln_g[i], conv_ln_b[i])
        y_gla = _gla(q, k, v, r, g_lr, gate_w_up[i], gate_b[i], gla_norm[i])
        h = h + jnp.concatenate([y_conv, y_gla], axis=-1) @ w_out[i]
        h = h + 0.5 * _swiglu(_rmsnorm(h, ffn2_norm[i]), ffn2_w_in[i], ffn2_w_out[i])
        gate = jax.nn.sigmoid(_rmsnorm(h, ple_norm[i]) @ ple_w_gate[i])
        h = h + gate * (p[i] @ ple_w_proj[i])
    return _rmsnorm(h, final_norm)


def setup_inputs(seed=0):
    out = dict(first_inputs(seed))
    for name, value in second_inputs(seed + 1).items():
        if name != "x":
            out[name + "_2"] = value
    return out


def reference(
    x, mem, ffn1_norm, ffn1_w_gate, ffn1_w_up, ffn1_w_down, mix_norm, ev_w_in, ev_conv_w,
    ev_sinks, ev_w_out, od_w_in, od_w_out, rel_bias, xa_norm, xa_w_q, xa_w_kv, xa_w_o, mem_norm,
    ffn2_norm, ffn2_w_gate, ffn2_w_up, ffn2_w_down, final_norm, p_2, ffn1_norm_2, ffn1_w_in_2,
    ffn1_w_out_2, mix_norm_2, w_in_2, conv_w_2, conv_b_2, conv_ln_g_2, conv_ln_b_2, gate_w_up_2,
    gate_b_2, gla_norm_2, w_out_2, ffn2_norm_2, ffn2_w_in_2, ffn2_w_out_2, ple_norm_2,
    ple_w_gate_2, ple_w_proj_2, final_norm_2,
):
    x = first_block(
        x, mem, ffn1_norm, ffn1_w_gate, ffn1_w_up, ffn1_w_down, mix_norm, ev_w_in, ev_conv_w,
        ev_sinks, ev_w_out, od_w_in, od_w_out, rel_bias, xa_norm, xa_w_q, xa_w_kv, xa_w_o,
        mem_norm, ffn2_norm, ffn2_w_gate, ffn2_w_up, ffn2_w_down, final_norm,
    )
    return second_block(
        x, p_2, ffn1_norm_2, ffn1_w_in_2, ffn1_w_out_2, mix_norm_2, w_in_2, conv_w_2, conv_b_2,
        conv_ln_g_2, conv_ln_b_2, gate_w_up_2, gate_b_2, gla_norm_2, w_out_2, ffn2_norm_2,
        ffn2_w_in_2, ffn2_w_out_2, ple_norm_2, ple_w_gate_2, ple_w_proj_2, final_norm_2,
    )


_drawn_inputs = setup_inputs


def setup_inputs(seed=0):
    import zlib

    import numpy as np

    out = dict(_drawn_inputs(seed))
    spreads = {}
    factors = {'ffn1_norm': 3.516,
     'ev_sinks': 4.247,
     'xa_norm': 8.0,
     'mem_norm': 8.0,
     'ffn2_norm': 5.214,
     'conv_b_2': 3.878,
     'conv_ln_g_2': 3.096,
     'conv_ln_b_2': 8.0,
     'gate_b_2': 3.905,
     'gla_norm_2': 3.432,
     'ffn2_norm_2': 3.567,
     'ple_norm_2': 7.155}
    for name, (base, spread) in spreads.items():
        noise = np.random.default_rng([zlib.crc32(name.encode()), seed]).standard_normal(out[name].shape)
        drawn = base * np.exp(spread * noise) if base else spread * noise
        out[name] = __import__('jax').numpy.asarray(drawn.astype(out[name].dtype))
    for name, factor in factors.items():
        out[name] = (out[name] * factor).astype(out[name].dtype)
    return out
```

```python
from contextlib import ExitStack

import numpy as np

import concourse.bass as bass
from concourse import mybir

P = 128
T = 256
NT = T // P
D = 1024
KD = D // P
FF = 2816
UC = 256
NJ = FF // UC
HALF = 1024
SWA_GROUPS = [(0, [0, 1, 2, 3], 128), (0, [4, 5, 6, 7], 128)] + [(1, [h, h + 1], 256) for h in (0, 2, 4, 6)]
MOBA_GROUPS = SWA_GROUPS
XA_GROUPS = [(t, [h, h + 1], 256) for t in range(2) for h in (0, 2)]
PROJ_BEFORE_2 = 9 + 6 + 12 + 2
RAW = 3
SPL = 6
LEAD = SPL - 1
EPS = 1e-6
MASKED = -1e38
ROWS, COLS, PAIRED, RANK = "rows", "cols", "paired", "rank"
GATE_RANK = 16
CONV_TAPS = 31

F32 = mybir.dt.float32
F32R = mybir.dt.float32r
U32 = mybir.dt.uint32
ALU = mybir.AluOpType
ACT = mybir.ActivationFunctionType
AX = mybir.AxisListType

COL_OF = {}
_at = 0
for _name, _n in (("ffn1", 16), ("mix", 16), ("xa", 16), ("ffn2", 16), ("mem", 8), ("ffn1_2", 8),
                  ("mix_2", 8), ("ffn2_2", 8), ("ple_2", 8), ("conv_w", 12), ("conv_b_2", 4),
                  ("ln_g_2", 4), ("ln_b_2", 4), ("conv_w_2", 124), ("gate_b_2", 2)):
    COL_OF[_name] = _at
    _at += _n
N_COLS = _at


def bucket_starts():
    d = np.arange(256)
    nf = np.maximum(d, 1).astype(np.float32)
    large = 16 + (np.log(nf / np.float32(16)) / np.float32(np.log(8.0)) * np.float32(16)).astype(np.int32)
    b = np.where(d < 16, d, np.minimum(large, 31))
    return [int(np.argmax(b == n)) for n in range(32)] + [256]


class Counter:

    def __init__(self, eng, sems):
        self.eng, self.sems, self.seen = eng, sems, {n: 0 for n in sems}

    def next(self, name, n=1):
        self.seen[name] += n
        self.eng.wait_ge(self.sems[name], self.seen[name])

    def skip(self, name, n):
        self.seen[name] += n


def build(nc, a, out):
    w_all = {k: v for k, v in a.items()}

    units = []

    def col_unit(w, c0):
        units.append((COLS, w.rearrange("(k p) f -> p k f", p=P)[:, :, c0:c0 + UC]))

    def row_unit(w, r0):
        units.append((ROWS, w[r0:r0 + UC, :].rearrange("(s p) n -> p s n", p=P)))

    def ffn_units(gate, up, down):
        col_unit(gate, 0)
        col_unit(up, 0)
        for j in range(1, NJ):
            col_unit(gate, j * UC)
            col_unit(up, j * UC)
            row_unit(down, (j - 1) * UC)
        row_unit(down, (NJ - 1) * UC)

    ffns = []

    def ffn(gate, up, down):
        ffns.append((len(units), gate, up, down))
        ffn_units(gate, up, down)

    def cols_of(w, c0, n):
        for c in range(c0, c0 + n, UC):
            col_unit(w, c)

    def rows_of(w):
        for r in range(0, w.shape[0], UC):
            row_unit(w, r)

    for l in range(2):
        ffn(a["ffn1_w_gate"][l], a["ffn1_w_up"][l], a["ffn1_w_down"][l])
        if l == 0:
            w = a["ev_w_in"][0]
            pairs = w[:, 1536:2048].rearrange("(k p) (h c) -> p k h c", p=P, h=2)
            for i in range(2):
                units.append((PAIRED, pairs[:, :, :, i * P:(i + 1) * P]))
            col_unit(w, 2048)
            for c in (512, 1024, 768, 1280, 0, 256):
                col_unit(w, c)
            rows_of(a["ev_w_out"][0])
            cols_of(a["xa_w_q"][l], 0, 512)
            cols_of(a["xa_w_kv"][l], 0, 1024)
        else:
            cols_of(a["od_w_in"][0], 0, 2048)
            cols_of(a["xa_w_kv"][l], 0, 1024)
            rows_of(a["od_w_out"][0])
            cols_of(a["xa_w_q"][l], 0, 512)
        rows_of(a["xa_w_o"][l])
        ffn(a["ffn2_w_gate"][l], a["ffn2_w_up"][l], a["ffn2_w_down"][l])
    w = a["ffn1_w_in_2"][0]
    ffn(w[:, 0:FF], w[:, FF:2 * FF], a["ffn1_w_out_2"][0])
    w = a["w_in_2"][0]
    units.append((RANK, w.rearrange("(k p) f -> p k f", p=P)[:, :, w.shape[1] - P:w.shape[1]]))
    for c in (1024, 1280, 0, 512, 256, 768, 1536, 1792, 2048, 2304):
        col_unit(w, c)
    rows_of(a["w_out_2"][0])
    w = a["ffn2_w_in_2"][0]
    ffn(w[:, 0:FF], w[:, FF:2 * FF], a["ffn2_w_out_2"][0])
    rows_of(a["ple_w_proj_2"][0])
    rows_of(a["ple_w_gate_2"][0])
    n_half = 2 * len(units)
    landed, in_slot = [], [0] * RAW
    for u, (kind, _) in enumerate(units):
        in_slot[u % RAW] += 32 if kind == PAIRED else 16
        landed.append(in_slot[u % RAW])

    with ExitStack() as ctx:
        def sb(name, shape, dt=F32):
            return ctx.enter_context(nc.sbuf_tensor(name, shape, dt))

        raw = sb("raw", [P, RAW, 2 * HALF])
        w_hi = sb("w_hi", [P, SPL, HALF], F32R)
        w_lo = sb("w_lo", [P, SPL, HALF], F32R)
        x = sb("x", [P, NT, D])
        xT_hi = sb("xT_hi", [P, KD, T], F32R)
        xT_lo = sb("xT_lo", [P, KD, T], F32R)
        yT_hi = sb("yT_hi", [P, KD, T], F32R)
        yT_lo = sb("yT_lo", [P, KD, T], F32R)
        memT_hi = sb("memT_hi", [P, KD, T], F32R)
        memT_lo = sb("memT_lo", [P, KD, T], F32R)
        hid_hi = sb("hid_hi", [P, 4, T], F32R)
        hid_lo = sb("hid_lo", [P, 4, T], F32R)
        arena = sb("arena", [P, 12288])
        bias = sb("bias", [P, 8, T])
        gain_row = sb("gain_row", [P, D])
        cols = sb("cols", [P, 256])
        ident = sb("ident", [P, P])
        small = sb("small", [P, 256])
        rank_w = sb("rank_w", [P, T])
        rank_x = sb("rank_x", [P, T])
        table = sb("table", [8, 32])
        spread = sb("spread", [8, 384])
        bank = ctx.enter_context(nc.psum_tensor("bank", [P, 8, 512], F32))

        mean_sq, rstd = small[:, 0:2], small[:, 2:4]
        sink, neg_sink = small[:, 8:16], small[:, 16:24]
        neg_max, top = small[:, 24:48], small[:, 48:72]
        den, inv = small[:, 72:96], small[:, 96:120]
        sink_in, sink_e = small[:, 120:144], small[:, 144:168]
        decay_in = small[:, 168:176]
        decay = small[:, 176:184]
        o_ms, o_rstd = small[:, 184:192], small[:, 192:200]

        mem_in = arena[:, 8192:10240].rearrange("p (t d) -> p t d", t=NT)
        xn = arena[:, 0:2048].rearrange("p (t d) -> p t d", t=NT)
        prob = arena[:, 0:3072].rearrange("p (g c) -> p g c", c=512)
        probT = arena[:, 3072:6144].rearrange("p (g c) -> p g c", c=512)
        act_gate = arena[:, 3072:4096].rearrange("p (j c) -> p j c", j=2)
        hidden = arena[:, 4096:5120].rearrange("p (j c) -> p j c", j=2)
        q_sb = arena[:, 6144:8192].rearrange("p (h t) -> p h t", t=T)
        k_sb = arena[:, 8192:9216].rearrange("p (h t) -> p h t", t=T)
        v_sb = arena[:, 9216:10240].rearrange("p (t d) -> p t d", t=NT)
        mem_k = arena[:, 10240:11264].rearrange("p (h t) -> p h t", t=T)
        mem_v = arena[:, 11264:12288].rearrange("p (t d) -> p t d", t=NT)
        bias_rev = arena[:, 10240:12288].rearrange("p (h c) -> p h c", h=8)
        flip = arena[:, 5120:5248]
        col_rows = arena[:, 5248:5504].rearrange("p (a c) -> p a c", a=2)
        swa_k, swa_v = k_sb[:, 0, :], arena[:, 9216:9472].rearrange("p (t d) -> p t d", t=NT)
        conv_c = arena[:, 7168:8192].rearrange("p (n c) -> p n c", n=2)
        conv_u = arena[:, 8448:8960]
        conv_v = arena[:, 9472:9988].rearrange("p (n c) -> p n c", n=2)
        conv_b = arena[:, 10240:11264].rearrange("p (n c) -> p n c", n=2)
        conv_y = arena[:, 11264:12288].rearrange("p (n c) -> p n c", n=2)
        PAD = CONV_TAPS - 1
        glu = arena[:, 0:4 * (T + PAD)].rearrange("p (n c) -> p n c", n=4)
        conv_acc = arena[:, 1152:2176].rearrange("p (n c) -> p n c", n=4)
        sig_b = arena[:, 2176:3200].rearrange("p (n c) -> p n c", n=4)
        centred = arena[:, 2176:3200].rearrange("p (n c) -> p n c", n=4)
        g_q, g_k = arena[:, 3200:3712], arena[:, 3712:4224]
        g_v = arena[:, 4224:5248].rearrange("p (t d) -> p t d", t=NT)
        g_r = arena[:, 5248:6272].rearrange("p (t d) -> p t d", t=NT)
        g_z, g_l, g_cum = arena[:, 6272:6784], arena[:, 6784:7296], arena[:, 7296:7808]
        e_pos, e_neg, e_end = arena[:, 7808:8320], arena[:, 8320:8832], arena[:, 8832:9344]
        q_dec, q_neg = g_z, g_l
        k_neg, k_pos, k_end = arena[:, 9344:9856], arena[:, 9856:10368], arena[:, 10368:10880]
        k_nat = e_pos
        score = arena[:, 10880:11904].rearrange("p (h c) -> p h c", h=2)
        ones = arena[:, 11904:12032]
        ln_rstd = e_end[:, 0:T]
        low_mask, up_mask = arena[:, 12032:12160], arena[:, 12160:12288]
        state = bias[:, 0:3, :]
        reset = bias[:, 3, :]
        gla_gain = bias[:, 4:6, :].rearrange("p a c -> p (a c)")
        sq_c = arena[:, 0:1024].rearrange("p (n c) -> p n c", n=4)
        o_nat = arena[:, 9344:10368].rearrange("p (t d) -> p t d", t=NT)
        p_in = arena[:, 6144:6656].rearrange("p (t c) -> p t c", t=NT)
        p_out = arena[:, 7168:9216].rearrange("p (t d) -> p t d", t=NT)
        ple_gate = arena[:, 9216:11264].rearrange("p (t d) -> p t d", t=NT)

        spread_dram = nc.dram_tensor("spread_dram", [8, 384], F32).ap()
        bias_dram = nc.dram_tensor("bias_dram", [P, 8 * T], F32).ap()

        names = """vectors_loaded x_loaded mem_loaded table_loaded sinks_loaded gain_loaded rank_loaded
            p_loaded gla_gain_loaded spread_stored bias_rev_loaded bias_stored bias_loaded out_stored
            pool_const spread_ready bias_masked gla_const rank_zero
            vectors_psum cols_ready bias_psum bias_ready
            hi_ready lo_ready half_done
            residual mean_sq normed xT_psum xT_hi_ready xT_lo_ready acc_ready
            act_gate_ready hidden_ready hidden_hi_ready hidden_lo_ready
            proj_sb scores max_ready exp_ready probs_ready probT_psum probT_even probT_odd
            out_psum y_hi_ready y_lo_ready conv_v_ready conv_ready conv_tap dve_step act_step
            rank_psum decays gla_operands gla_scores score_ready kv_psum states_ready ln_ready
            k_nat_psum k_nat_ready o_square gated mean_psum var_in var_psum result_ready""".split()
        sem = {n: ctx.enter_context(nc.semaphore(n)) for n in names}
        raw_ready = [ctx.enter_context(nc.semaphore(f"raw_ready{i}")) for i in range(RAW)]
        block = ctx.enter_context(nc.Block())

        def d_bank(t, n):
            return bank[:, 4 + 2 * t + n, :]

        def raw_half(v):
            kind = units[v // 2][0]
            slot = raw[:, (v // 2) % RAW, :]
            hi, lo = w_hi[:, v % SPL, :], w_lo[:, v % SPL, :]
            if kind == ROWS:
                return slot[:, (v % 2) * HALF:(v % 2 + 1) * HALF], hi, lo
            if kind == COLS:
                src = slot.rearrange("p (k f) -> p k f", k=KD)[:, :, (v % 2) * P:(v % 2 + 1) * P]
                return src, *(m.rearrange("p (k f) -> p k f", k=KD) for m in (hi, lo))
            if kind == PAIRED:
                src = slot.rearrange("p (h k i d) -> p i k h d", k=KD, h=2, i=2)[:, v % 2]
                return src, *(m.rearrange("p (k h d) -> p k h d", k=KD, h=2) for m in (hi, lo))
            return slot[:, (v % 2) * 512:(v % 2 + 1) * 512], hi[:, 0:512], lo[:, 0:512]

        FFN_HALVES = 2 * 3 * NJ
        LOOP_HALVES = 2 * 6
        LOOPS = (NJ - 3) // 2

        @block.sync
        def _(sp):
            def load(u, src, i=None):
                slot = u % RAW
                if u >= RAW:
                    ready = 2 * (u - RAW) + 2
                    sp.wait_ge(sem["lo_ready"], ready if i is None else ready + LOOP_HALVES * i)
                kind = units[u][0]
                if kind == RANK:
                    dst = raw[:, slot, 0:HALF].rearrange("p (k f) -> p k f", k=KD)
                elif kind == PAIRED:
                    for h in range(2):
                        dst = raw[:, slot, h * HALF:(h + 1) * HALF].rearrange("p (k c) -> p k c", k=KD)
                        sp.dma_start(dst, src[:, :, h, :]).then_inc(raw_ready[slot], 16)
                    return
                elif kind == ROWS:
                    dst = raw[:, slot, :].rearrange("p (s n) -> p s n", s=2)
                else:
                    dst = raw[:, slot, :].rearrange("p (k f) -> p k f", k=KD)
                sp.dma_start(dst, src).then_inc(raw_ready[slot], 16)

            sp.dma_start(x[:, :, :], a["x"][0].rearrange("(t p) d -> p t d", p=P)).then_inc(sem["x_loaded"], 16)
            u = 0
            done = 0
            while u < len(units):
                if done < len(ffns) and u == ffns[done][0]:
                    _, gate, up, down = ffns[done]
                    done += 1
                    gate_v, up_v = (m.rearrange("(k p) f -> p k f", p=P) for m in (gate, up))
                    for n in range(5):
                        load(u + n, units[u + n][1])
                    with sp.Fori(0, LOOPS) as i:
                        for s in range(2):
                            c0 = i * (2 * UC) + (2 + s) * UC
                            load(u + 5 + 3 * s, gate_v[:, :, bass.ds(c0, UC)], i)
                            load(u + 6 + 3 * s, up_v[:, :, bass.ds(c0, UC)], i)
                            r0 = i * (2 * UC) + (1 + s) * UC
                            load(u + 7 + 3 * s, down[bass.ds(r0, UC), :].rearrange("(s p) n -> p s n", p=P), i)
                    for n in range(5 + 6 * LOOPS, 3 * NJ):
                        load(u + n, units[u + n][1])
                    u += 3 * NJ
                else:
                    load(u, units[u][1])
                    u += 1
            for t in range(NT):
                sp.wait_ge(sem["result_ready"], t + 1)
                sp.dma_start(out[0].rearrange("(t p) d -> p t d", p=P)[:, t, :], xn[:, t, :]).then_inc(sem["out_stored"], 16)
            sp.wait_ge(sem["out_stored"], 16 * NT)

        @block.gpsimd
        def _(pool):
            pool.memset(ident[:, :], 0.0).then_inc(sem["pool_const"], 1)
            pool.memset(flip, 0.0).then_inc(sem["pool_const"], 1)
            pool.memset(spread[:, :], MASKED).then_inc(sem["pool_const"], 1)
            pool.wait_ge(sem["pool_const"], 3)
            pool.affine_select(out=ident[:, :], in_=ident[:, :], compare_op=ALU.not_equal, fill=1.0, base=0,
                               pattern=[[-1, P]], channel_multiplier=1).then_inc(sem["pool_const"], 1)
            pool.affine_select(out=flip, in_=flip, compare_op=ALU.not_equal, fill=1.0, base=1 - P,
                               pattern=[[1, P]], channel_multiplier=1).then_inc(sem["pool_const"], 1)
            pool.memset(rank_w[:, :], 0.0).then_inc(sem["rank_zero"], 1)
            pool.wait_ge(sem["table_loaded"], 16)
            starts = bucket_starts()
            for b in range(32):
                lo, hi = 256 - starts[b + 1], 256 - starts[b]
                last = pool.tensor_copy(spread[:, lo:hi], table[:, b:b + 1].to_broadcast([8, hi - lo]))
                last.then_inc(sem["spread_ready"], 1)
            pool.wait_ge(sem["spread_ready"], 32)
            pool.dma_start(spread_dram, spread[:, :]).then_inc(sem["spread_stored"], 16)
            pool.wait_ge(sem["spread_stored"], 16)
            pool.dma_start(bias_rev, bass.AP(spread_dram.tensor, 0, [[1, P], [384, 8], [1, T]]))\
                .then_inc(sem["bias_rev_loaded"], 16)
            pool.wait_ge(sem["bias_ready"], 4)
            pool.dma_start(bias_dram, bias[:, :, :].rearrange("p h c -> p (h c)")).then_inc(sem["bias_stored"], 16)
            pool.wait_ge(sem["bias_stored"], 16)
            pool.affine_select(out=bias[:, :, :], in_=bias[:, :, :], compare_op=ALU.is_gt, fill=MASKED, base=0,
                               pattern=[[0, 8], [1, T]], channel_multiplier=-1).then_inc(sem["bias_masked"], 1)
            pool.wait_ge(sem["max_ready"], 6)
            pool.dma_start(bias[:, :, :].rearrange("p h c -> p (h c)"), bias_dram).then_inc(sem["bias_loaded"], 16)
            pool.wait_ge(sem["y_lo_ready"], 2 + 2 + 2 + 4 + 2)
            made = 0

            def constant(ins):
                nonlocal made
                made += 1
                ins.then_inc(sem["gla_const"], 1)
                pool.wait_ge(sem["gla_const"], made)

            for m, value in ((ones, 1.0 / 512), (low_mask, 1.0), (up_mask, 1.0), (reset, 1.0),
                             (score[:, :, :], 0.0)):
                constant(pool.memset(m, value))
            for m, mult, stp, base in ((low_mask, -1, 1, 1), (up_mask, 1, -1, 0)):
                constant(pool.affine_select(out=m, in_=m, compare_op=ALU.is_gt, fill=0.0, base=base,
                                            pattern=[[stp, P]], channel_multiplier=mult))
            constant(pool.memset(low_mask[0:64, 64:128], 0.0))
            constant(pool.memset(up_mask[64:128, 0:64], 0.0))
            constant(pool.memset(reset.rearrange("p (c n) -> p c n", n=64)[:, :, 0:1], 0.0))

        N_GLA_CONST = 5 + 2 + 3

        @block.scalar
        def _(act):
            c = Counter(act, sem)
            v_next = [0]

            def split(i=None, v=None):
                v = v_next[0] if v is None else v
                if v >= n_half:
                    return
                slot = (v // 2) % RAW
                if v % 2 == 0:
                    need = landed[v // 2]
                    act.wait_ge(raw_ready[slot], need if i is None else need + 16 * LOOP_HALVES // 2 // RAW * i)
                if v >= SPL:
                    need = v - SPL + 1
                    act.wait_ge(sem["half_done"], need if i is None else need + LOOP_HALVES * i)
                src, hi, _ = raw_half(v)
                act.activation(hi, src, ACT.Copy).then_inc(sem["hi_ready"], 1)
                if i is None:
                    v_next[0] += 1

            def splits(n):
                for _ in range(n):
                    split()

            def mean_squares(src=x, loaded=None):
                for t in range(NT):
                    if loaded is None:
                        c.next("residual")
                    else:
                        act.wait_ge(sem[loaded], 16)
                    act.activation(xn[:, t, :], src[:, t, :], ACT.Square, scale=1.0 / 32,
                                   accum_out=mean_sq[:, t:t + 1]).then_inc(sem["mean_sq"], 1)

            def norm(gain, hi, src=x, loaded=None):
                mean_squares(src, loaded)
                xT_his(gain, hi)

            def xT_his(gain, hi):
                for b in range(KD // 2):
                    c.next("xT_psum")
                    for k in (2 * b, 2 * b + 1):
                        last = act.activation(hi[:, k, :], bank[:, b, (k % 2) * T:(k % 2 + 1) * T], ACT.Copy,
                                              scale=cols[:, gain + k:gain + k + 1])
                    last.then_inc(sem["xT_hi_ready"], 1)
            def ffn_step(f, j, i=None):
                g_half = f.v0 + (4 + 6 * (j - 1) if j else 0)
                plus = (lambda k, n: k if i is None else k + n * i)
                jb = j % 2
                act.wait_ge(sem["half_done"], plus(g_half + 2, LOOP_HALVES))
                act.activation(act_gate[:, jb, :], bank[:, 2 * jb, :], ACT.Silu).then_inc(sem["act_gate_ready"], 1)
                n_splits = 6 if 0 < j < NJ - 1 else (4 if j == 0 else 8)
                base = g_half + LEAD
                for n in range(4 if j else 2):
                    split(i, base + n)
                act.wait_ge(sem["hidden_ready"], plus(f.j0 + j + 1, 2))
                act.activation(hid_hi[:, 2 * jb:2 * jb + 2, :], hidden[:, jb, :].rearrange("p (s t) -> p s t", s=2),
                               ACT.Copy).then_inc(sem["hidden_hi_ready"], 1)
                for n in range(4 if j else 2, n_splits):
                    split(i, base + n)
                if i is None:
                    v_next[0] = base + n_splits

            class Ffn:
                pass

            n_ffn = [0]

            def ffn():
                f = Ffn()
                f.v0, f.j0 = 2 * ffns[n_ffn[0]][0], NJ * n_ffn[0]
                assert v_next[0] == f.v0 + LEAD
                n_ffn[0] += 1
                ffn_step(f, 0)
                ffn_step(f, 1)
                with act.Fori(0, LOOPS) as i:
                    ffn_step(f, 2, i)
                    ffn_step(f, 3, i)
                ffn_step(f, NJ - 1)
                assert v_next[0] == f.v0 + FFN_HALVES + LEAD

            def evac(n, dst, b, func=ACT.Copy, src=None):
                act.wait_ge(sem["half_done"], n)
                src = bank[:, b, :] if src is None else src
                act.activation(dst, src, func).then_inc(sem["proj_sb"], 1)

            def halves(m):
                return m.rearrange("p (s t) -> p s t", s=2)

            def softmax_exp(groups, sinks, scale=1.0, from_psum=False):
                for g, (t, heads, nk) in enumerate(groups):
                    c.next("max_ready")
                    for n in range(len(heads)):
                        m = 4 * g + n
                        dst = prob[:, g, n * nk:(n + 1) * nk]
                        src = bank[:, g, n * nk:(n + 1) * nk] if from_psum else dst
                        last = act.activation(dst, src, ACT.Exp, bias=neg_max[:, m:m + 1], scale=scale,
                                              accum_out=den[:, m:m + 1])
                    if sinks:
                        nh = len(heads)
                        last = act.activation(sink_e[:, 4 * g:4 * g + nh], sink_in[:, 4 * g:4 * g + nh], ACT.Exp)
                    last.then_inc(sem["exp_ready"], 1)
                    yield g

            def probT_copies(groups, which):
                for g in range(len(groups)):
                    c.next("probT_psum")
                    if g % 2 == which:
                        act.activation(probT[:, g, :], bank[:, (len(groups) + g) % 8, :], ACT.Copy)\
                            .then_inc(sem["probT_even"], 1)

            def y_hi(n_banks, dst):
                for n in range(n_banks):
                    c.next("out_psum")
                    d, s = dst(n)
                    act.activation(d, s, ACT.Copy).then_inc(sem["y_hi_ready"], 1)

            at = 0
            srcs = [("ffn1_norm", 16), ("mix_norm", 16), ("xa_norm", 16), ("ffn2_norm", 16), ("mem_norm", 8),
                    ("ffn1_norm_2", 8), ("mix_norm_2", 8), ("ffn2_norm_2", 8), ("ple_norm_2", 8),
                    ("ev_conv_w", 12), ("conv_b_2", 4), ("conv_ln_g_2", 4), ("conv_ln_b_2", 4),
                    ("conv_w_2", 124), ("gate_b_2", 2)]
            for name, n in srcs:
                ap = a[name]
                dims = "abc"[:len(ap.shape)]
                flat = ap.rearrange(f"{' '.join(dims)} -> ({' '.join(dims)})") if len(dims) > 1 else ap
                act.dma_start(col_rows[at % P:at % P + n, at // P, :], flat.rearrange("(r c) -> r c", c=P))\
                    .then_inc(sem["vectors_loaded"], 16)
                at += n
            act.dma_start(mem_in[:, :, :], a["mem"][0].rearrange("(t p) d -> p t d", p=P)).then_inc(sem["mem_loaded"], 16)
            with nc.allow_non_contiguous_dma(reason="32 x 8 table"):
                act.dma_start(table[:, :], a["rel_bias"].rearrange("b h -> h b")).then_inc(sem["table_loaded"], 16)
            act.dma_start(sink, a["ev_sinks"].to_broadcast([P, 8])).then_inc(sem["sinks_loaded"], 16)
            act.dma_start(gain_row[:, :], a["final_norm"].rearrange("(a n) -> a n", a=1).to_broadcast([P, D]))\
                .then_inc(sem["gain_loaded"], 16)
            act.wait_ge(sem["rank_zero"], 1)
            act.dma_start(rank_w[P - GATE_RANK:P, :], a["gate_w_up_2"][0]).then_inc(sem["rank_loaded"], 16)

            norm(COL_OF["mem"], memT_hi, mem_in, "mem_loaded")
            mean_squares(x, "x_loaded")
            splits(LEAD)
            xT_his(COL_OF["ffn1"], xT_hi)
            ffn()
            norm(COL_OF["mix"], xT_hi)
            v = v_next[0] - LEAD
            evac(v + 2, q_sb[:, 0:2, :], 0, src=halves(bank[:, 0, :]))
            splits(2)
            evac(v + 4, q_sb[:, 2:4, :], 1, src=halves(bank[:, 1, :]))
            splits(2)
            act.wait_ge(sem["half_done"], v + 6)
            act.activation(swa_k, bank[:, 2, 0:T], ACT.Copy)
            act.activation(swa_v, bank[:, 2, T:2 * T].rearrange("p (t d) -> p t d", t=NT), ACT.Copy).then_inc(sem["proj_sb"], 1)
            splits(2)
            soft = softmax_exp(SWA_GROUPS, True)
            evac(v + 8, conv_c[:, 0, :], 6)
            splits(2)
            evac(v + 10, conv_u, 7)
            splits(2)
            next(soft)
            next(soft)
            evac(v + 12, conv_c[:, 1, :], 6)
            splits(2)
            next(soft)
            act.wait_ge(sem["conv_v_ready"], 1)
            evac(v + 14, conv_u, 7)
            splits(2)
            next(soft)
            evac(v + 16, conv_b[:, 0, :], 6)
            splits(2)
            next(soft)
            evac(v + 18, conv_b[:, 1, :], 7)
            splits(2)
            next(soft)
            for n in range(2):
                act.wait_ge(sem["conv_ready"], n + 1)
                act.activation(yT_hi[:, 2 * n:2 * n + 2, :], halves(conv_y[:, n, :]), ACT.Copy).then_inc(sem["y_hi_ready"], 1)
            probT_copies(SWA_GROUPS, 0)
            y_hi(2, lambda n: (yT_hi[:, 4:8, n * P:(n + 1) * P], bank[:, 4 + n, :].rearrange("p (i q) -> p i q", i=4)))
            splits(8)

            def cross(l, kv):
                norm(COL_OF["xa"] + KD * l, xT_hi)
                v = v_next[0] - LEAD
                for n in range(2):
                    evac(v + 2 + 2 * n, q_sb[:, 2 * n:2 * n + 2, :], n, src=halves(bank[:, n, :]))
                    splits(2)
                if kv:
                    mem_kv(2)
                for _ in softmax_exp(XA_GROUPS, False, 128.0 ** -0.5, from_psum=True):
                    pass
                probT_copies(XA_GROUPS, 0)
                y_hi(2, lambda n: (yT_hi[:, 0:4, n * P:(n + 1) * P], bank[:, n, :].rearrange("p (i q) -> p i q", i=4)))
                splits(4)

            def mem_kv(b0, between=lambda: None):
                v = v_next[0] - LEAD
                for n in range(4):
                    b = b0 + n % 2 if b0 == 6 else b0 + n
                    if n < 2:
                        evac(v + 2 + 2 * n, mem_k[:, 2 * n:2 * n + 2, :], b, src=halves(bank[:, b, :]))
                    else:
                        evac(v + 2 + 2 * n, mem_v[:, :, (n - 2) * T:(n - 1) * T], b, src=halves(bank[:, b, :]))
                    splits(2)
                    between()

            cross(0, True)
            norm(COL_OF["ffn2"], xT_hi)
            ffn()
            norm(COL_OF["ffn1"] + KD, xT_hi)
            ffn()
            norm(COL_OF["mix"] + KD, xT_hi)
            v = v_next[0] - LEAD
            for n in range(8):
                dst = (q_sb[:, 2 * n:2 * n + 2, :] if n < 4 else k_sb[:, 2 * n - 8:2 * n - 6, :] if n < 6
                       else v_sb[:, :, (n - 6) * T:(n - 5) * T])
                evac(v + 2 + 2 * n, dst, n, src=halves(bank[:, n, :]))
                splits(2)
            soft = softmax_exp(MOBA_GROUPS, False)
            mem_kv(6, lambda: next(soft))
            for _ in soft:
                pass
            probT_copies(MOBA_GROUPS, 0)
            y_hi(4, lambda n: (yT_hi[:, 4 * (n % 2):4 * (n % 2) + 4, (n // 2) * P:(n // 2 + 1) * P],
                               bank[:, 4 + n, :].rearrange("p (i q) -> p i q", i=4)))
            splits(8)
            cross(1, False)
            norm(COL_OF["ffn2"] + KD, xT_hi)
            ffn()
            mean_squares()
            mean_squares()
            act.dma_start(gain_row[:, :], a["final_norm_2"].rearrange("(a n) -> a n", a=1).to_broadcast([P, D]))\
                .then_inc(sem["gain_loaded"], 16)
            act.dma_start(gla_gain, a["gla_norm_2"].to_broadcast([P, 512])).then_inc(sem["gla_gain_loaded"], 16)
            xT_his(COL_OF["ffn1_2"], xT_hi)
            ffn()
            norm(COL_OF["mix_2"], xT_hi)
            v = v_next[0] - LEAD
            evac(v + 2, rank_x[:, :], 0, src=bank[:, 0, 0:T])
            splits(2)
            evac(v + 4, g_q, 5)
            splits(2)
            c.next("decays")
            act.activation(g_l, g_l, ACT.Exp).then_inc(sem["act_step"], 1)
            c.next("act_step")
            act.activation(g_l, g_l, ACT.Ln, bias=1.0).then_inc(sem["act_step"], 1)
            c.next("act_step")
            evac(v + 6, g_k, 6)
            splits(2)
            c.next("decays")
            act.activation(e_pos, g_cum, ACT.Exp, scale=1.0 / 16)
            act.activation(e_neg, g_cum, ACT.Exp, scale=-1.0 / 16).then_inc(sem["act_step"], 1)
            c.next("act_step")
            c.next("decays")
            act.activation(e_end, e_end, ACT.Exp, scale=1.0 / 16)
            act.activation(decay, decay_in, ACT.Exp, scale=1.0 / 16).then_inc(sem["act_step"], 1)
            c.next("act_step")
            for n in range(2):
                evac(v + 8 + 4 * n, glu[:, 2 * n:2 * n + 2, PAD:PAD + T], 1 + 2 * n, src=halves(bank[:, 1 + 2 * n, :]))
                splits(2)
                evac(v + 10 + 4 * n, sig_b[:, 2 * n:2 * n + 2, :], 2 + 2 * n, func=ACT.Sigmoid,
                     src=halves(bank[:, 2 + 2 * n, :]))
                splits(2)
            for n in range(2):
                evac(v + 16 + 2 * n, g_v[:, :, n * T:(n + 1) * T], (7, 0)[n], src=halves(bank[:, (7, 0)[n], :]))
                splits(2)
            for n in range(2):
                evac(v + 20 + 2 * n, g_r[:, :, n * T:(n + 1) * T], 1 + n, func=ACT.Silu, src=halves(bank[:, 1 + n, :]))
                splits(2)
            c.next("k_nat_psum")
            act.activation(k_nat, bank[:, 4, :], ACT.Copy).then_inc(sem["k_nat_ready"], 1)
            c.next("var_in")
            act.activation(sq_c[:, :, :], centred[:, :, :], ACT.Square).then_inc(sem["var_in"], 1)
            c.next("out_psum")
            for h in range(2):
                act.activation(score[:, h, :], bank[:, h, :], ACT.Square).then_inc(sem["o_square"], 1)
            c.next("ln_ready")
            for n in range(4):
                g, b = COL_OF["ln_g_2"] + n, COL_OF["ln_b_2"] + n
                last = act.activation(conv_acc[:, n, :], centred[:, n, :], ACT.Silu, scale=cols[:, g:g + 1],
                                      bias=cols[:, b:b + 1])
            last.then_inc(sem["act_step"], 1)
            c.next("act_step")
            act.activation(yT_hi[:, 0:4, :], conv_acc[:, :, :], ACT.Copy).then_inc(sem["y_hi_ready"], 1)
            y_hi(2, lambda n: (yT_hi[:, 4 + 2 * n:6 + 2 * n, :], halves(bank[:, 2 + n, :])))
            splits(8)
            mean_squares()
            act.dma_start(p_in[:, :, :], a["p_2"][0, 0].rearrange("(t p) c -> p t c", p=P)).then_inc(sem["p_loaded"], 16)
            xT_his(COL_OF["ffn2_2"], xT_hi)
            ffn()
            norm(COL_OF["ple_2"], xT_hi)
            y_hi(1, lambda n: (yT_hi[:, 0:2, :], halves(bank[:, 0, :])))
            v = v_next[0] - LEAD
            act.wait_ge(sem["half_done"], v + 2)
            for t in range(NT):
                act.activation(p_out[:, t, :], bank[:, 2 * t:2 * t + 2, :].rearrange("p a c -> p (a c)"), ACT.Copy)\
                    .then_inc(sem["proj_sb"], 1)
            splits(10)
            for t in range(NT):
                act.wait_ge(sem["half_done"], n_half)
                act.activation(ple_gate[:, t, :], bank[:, 4 + 2 * t:6 + 2 * t, :].rearrange("p a c -> p (a c)"),
                               ACT.Sigmoid).then_inc(sem["proj_sb"], 1)
            mean_squares()

        @block.vector
        def _(dve):
            c = Counter(dve, sem)
            v_next = [0]

            def link(ins, name="dve_step"):
                ins.then_inc(sem[name], 1)
                c.next(name)

            def split(i=None, v=None):
                v = v_next[0] if v is None else v
                if v >= n_half:
                    return
                dve.wait_ge(sem["hi_ready"], v + 1 if i is None else v + 1 + LOOP_HALVES * i)
                src, hi, lo = raw_half(v)
                dve.tensor_tensor(lo, src, hi.bitcast(F32), ALU.subtract).then_inc(sem["lo_ready"], 1)
                if i is None:
                    v_next[0] += 1

            def splits(n):
                for _ in range(n):
                    split()

            def rsqrt(dst, src, tmp):
                link(dve.tensor_scalar(src, src, EPS, None, ALU.add))
                link(dve.tensor_scalar(tmp.bitcast(U32), src.bitcast(U32), 1, None, ALU.logical_shift_right))
                link(dve.tensor_scalar(dst.bitcast(U32), tmp.bitcast(U32), -1.0, float(0x5F3759DF), ALU.mult, ALU.add))
                for _ in range(4):
                    link(dve.tensor_tensor(tmp, dst, dst, ALU.mult))
                    link(dve.scalar_tensor_tensor(tmp, tmp, -0.5, src, ALU.mult, ALU.mult))
                    link(dve.scalar_tensor_tensor(dst, tmp, 1.5, dst, ALU.add, ALU.mult))

            def rstd_of_both():
                c.next("mean_sq", 2)
                rsqrt(rstd, mean_sq, small[:, 4:6])

            def norm(gain, hi, lo, src=x):
                rstd_of_both()
                for t in range(NT):
                    dve.tensor_scalar(xn[:, t, :], src[:, t, :], rstd[:, t:t + 1], None, ALU.mult)\
                        .then_inc(sem["normed"], 1)
                for b in range(KD // 2):
                    c.next("xT_hi_ready")
                    for k in (2 * b, 2 * b + 1):
                        last = dve.scalar_tensor_tensor(lo[:, k, :], bank[:, b, (k % 2) * T:(k % 2 + 1) * T],
                                                        cols[:, gain + k:gain + k + 1], hi[:, k, :].bitcast(F32),
                                                        ALU.mult, ALU.subtract)
                    last.then_inc(sem["xT_lo_ready"], 1)

            def add_residual(scale, n_done):
                for t in range(NT):
                    if t == 0:
                        c.next("acc_ready")
                    else:
                        dve.wait_ge(sem["half_done"], n_done)
                    dve.scalar_tensor_tensor(x[:, t, :], bank[:, 4 + 2 * t:6 + 2 * t, :].rearrange("p a c -> p (a c)"),
                                             scale, x[:, t, :], ALU.mult, ALU.add).then_inc(sem["residual"], 1)

            def ffn_step(f, j, i=None):
                g_half = f.v0 + (4 + 6 * (j - 1) if j else 0)
                plus = (lambda k, n: k if i is None else k + n * i)
                jb = j % 2
                n_splits = 6 if 0 < j < NJ - 1 else (4 if j == 0 else 8)
                base = g_half + LEAD
                for n in range(2):
                    split(i, base + n)
                dve.wait_ge(sem["act_gate_ready"], plus(f.j0 + j + 1, 2))
                dve.wait_ge(sem["half_done"], plus(g_half + 4, LOOP_HALVES))
                dve.tensor_tensor(hidden[:, jb, :], act_gate[:, jb, :], bank[:, 2 * jb + 1, :], ALU.mult)\
                    .then_inc(sem["hidden_ready"], 1)
                for n in range(2, 4 if j else 2):
                    split(i, base + n)
                dve.wait_ge(sem["hidden_hi_ready"], plus(f.j0 + j + 1, 2))
                dve.tensor_tensor(hid_lo[:, 2 * jb:2 * jb + 2, :], hidden[:, jb, :].rearrange("p (s t) -> p s t", s=2),
                                  hid_hi[:, 2 * jb:2 * jb + 2, :].bitcast(F32), ALU.subtract)\
                    .then_inc(sem["hidden_lo_ready"], 1)
                for n in range(4 if j else 2, n_splits):
                    split(i, base + n)
                if i is None:
                    v_next[0] = base + n_splits

            class Ffn:
                pass

            n_ffn = [0]

            def ffn():
                f = Ffn()
                f.v0, f.j0 = 2 * ffns[n_ffn[0]][0], NJ * n_ffn[0]
                n_ffn[0] += 1
                ffn_step(f, 0)
                ffn_step(f, 1)
                with dve.Fori(0, LOOPS) as i:
                    ffn_step(f, 2, i)
                    ffn_step(f, 3, i)
                ffn_step(f, NJ - 1)
                add_residual(0.5, f.v0 + FFN_HALVES)

            def halves(m):
                return m.rearrange("p (s t) -> p s t", s=2)

            def logits(groups, sinks, scale, biased):
                for g, (t, heads, nk) in enumerate(groups):
                    c.next("scores")
                    nh = len(heads)
                    m = slice(4 * g, 4 * g + nh)
                    if biased:
                        dst = prob[:, g, :].rearrange("p (h k) -> p h k", k=nk)
                        link(dve.scalar_tensor_tensor(dst, bank[:, g, :].rearrange("p (h k) -> p h k", k=nk), scale,
                                                      bias[:, heads[0]:heads[0] + nh, T - nk:T], ALU.mult, ALU.add))
                        link(dve.tensor_reduce(top[:, m], dst, AX.X, ALU.max))
                    else:
                        link(dve.tensor_reduce(top[:, m], bank[:, g, :].rearrange("p (h k) -> p h k", k=nk), AX.X,
                                               ALU.max))
                    if sinks:
                        link(dve.scalar_tensor_tensor(neg_max[:, m], top[:, m], -1.0,
                                                      neg_sink[:, heads[0]:heads[0] + nh], ALU.mult, ALU.min))
                        dve.tensor_tensor(sink_in[:, m], sink[:, heads[0]:heads[0] + nh], neg_max[:, m], ALU.add)\
                            .then_inc(sem["max_ready"], 1)
                    else:
                        dve.tensor_scalar(neg_max[:, m], top[:, m], -1.0 if biased else -scale, None, ALU.mult)\
                            .then_inc(sem["max_ready"], 1)
                    yield g

            def normalise(groups, sinks):
                for g, (t, heads, nk) in enumerate(groups):
                    c.next("exp_ready")
                    nh = len(heads)
                    m = slice(4 * g, 4 * g + nh)
                    if sinks:
                        link(dve.tensor_tensor(den[:, m], den[:, m], sink_e[:, m], ALU.add))
                    link(dve.reciprocal(inv[:, m], den[:, m]))
                    for n in range(nh):
                        p = prob[:, g, n * nk:(n + 1) * nk]
                        last = dve.tensor_scalar(p, p, inv[:, 4 * g + n:4 * g + n + 1], None, ALU.mult)
                    last.then_inc(sem["probs_ready"], 1)
                    yield g

            def probT_copies(groups, which):
                for g in range(len(groups)):
                    c.next("probT_psum")
                    if g % 2 == which:
                        dve.tensor_copy(probT[:, g, :], bank[:, (len(groups) + g) % 8, :]).then_inc(sem["probT_odd"], 1)

            def y_lo(n_banks, dst):
                for n in range(n_banks):
                    c.next("y_hi_ready")
                    lo, src, hi = dst(n)
                    dve.tensor_tensor(lo, src, hi.bitcast(F32), ALU.subtract).then_inc(sem["y_lo_ready"], 1)

            c.next("vectors_psum")
            link(dve.tensor_copy(cols[:, 0:N_COLS], bank[:, 7, 0:N_COLS]), "cols_ready")
            dve.wait_ge(sem["sinks_loaded"], 16)
            link(dve.tensor_scalar(neg_sink, sink, -1.0, None, ALU.mult))
            norm(COL_OF["mem"], memT_hi, memT_lo, src=mem_in)
            splits(LEAD)
            norm(COL_OF["ffn1"], xT_hi, xT_lo)
            ffn()
            for n in range(4):
                c.next("bias_psum")
                dve.tensor_copy(bias[:, 2 * n:2 * n + 2, :], halves(bank[:, n, :])).then_inc(sem["bias_ready"], 1)
            norm(COL_OF["mix"], xT_hi, xT_lo)
            v = v_next[0] - LEAD
            for n in range(2):
                link(dve.memset(conv_v[:, n, 0:2], 0.0))
            splits(6)
            dve.wait_ge(sem["bias_masked"], 1)
            soft = logits(SWA_GROUPS, True, 0.125, True)
            norms = normalise(SWA_GROUPS, True)
            P0 = 3

            def conv(n, wait_cu):
                dve.wait_ge(sem["proj_sb"], wait_cu)
                dve.tensor_tensor(conv_v[:, :, 2:2 + T], halves(conv_c[:, n, :]), halves(conv_u), ALU.mult)\
                    .then_inc(sem["conv_v_ready"], 1)
                c.next("conv_v_ready")
                y = halves(conv_y[:, n, :])
                w = COL_OF["conv_w"]
                for i in range(2):
                    ch = 2 * n + i
                    link(dve.tensor_scalar(y[:, i, :], conv_v[:, i, 0:T], cols[:, w + ch:w + ch + 1], None, ALU.mult))
                    for j in (1, 2):
                        wj = w + 4 * j + ch
                        link(dve.scalar_tensor_tensor(y[:, i, :], conv_v[:, i, j:j + T], cols[:, wj:wj + 1],
                                                      y[:, i, :], ALU.mult, ALU.add))

            splits(4)
            next(soft)
            next(soft)
            conv(0, P0 + 2)
            next(soft)
            splits(2)
            next(soft)
            next(norms)
            splits(2)
            next(soft)
            next(soft)
            next(norms)
            splits(2)
            next(norms)
            conv(1, P0 + 4)
            next(norms)
            splits(2)
            next(norms)
            for n in range(2):
                dve.wait_ge(sem["proj_sb"], P0 + 5 + n)
                dve.tensor_tensor(conv_y[:, n, :], conv_y[:, n, :], conv_b[:, n, :], ALU.mult)\
                    .then_inc(sem["conv_ready"], 1)
            next(norms)
            y_lo(2, lambda n: (yT_lo[:, 2 * n:2 * n + 2, :], halves(conv_y[:, n, :]), yT_hi[:, 2 * n:2 * n + 2, :]))
            probT_copies(SWA_GROUPS, 1)
            y_lo(2, lambda n: (yT_lo[:, 4:8, n * P:(n + 1) * P], bank[:, 4 + n, :].rearrange("p (i q) -> p i q", i=4),
                               yT_hi[:, 4:8, n * P:(n + 1) * P]))
            v = v_next[0] - LEAD
            splits(8)
            add_residual(1.0, v + 8)

            def cross(l, kv):
                norm(COL_OF["xa"] + KD * l, xT_hi, xT_lo)
                splits(4)
                if kv:
                    splits(8)
                for _ in logits(XA_GROUPS, False, 128.0 ** -0.5, False):
                    pass
                for _ in normalise(XA_GROUPS, False):
                    pass
                probT_copies(XA_GROUPS, 1)
                y_lo(2, lambda n: (yT_lo[:, 0:4, n * P:(n + 1) * P], bank[:, n, :].rearrange("p (i q) -> p i q", i=4),
                                   yT_hi[:, 0:4, n * P:(n + 1) * P]))
                v = v_next[0] - LEAD
                splits(4)
                add_residual(1.0, v + 4)

            cross(0, True)
            norm(COL_OF["ffn2"], xT_hi, xT_lo)
            ffn()
            norm(COL_OF["ffn1"] + KD, xT_hi, xT_lo)
            ffn()
            norm(COL_OF["mix"] + KD, xT_hi, xT_lo)
            splits(16)
            dve.wait_ge(sem["bias_loaded"], 16)
            soft = logits(MOBA_GROUPS, False, 128.0 ** -0.5, True)
            norms = normalise(MOBA_GROUPS, False)
            next(soft)
            next(soft)
            splits(2)
            next(soft)
            next(norms)
            splits(2)
            next(soft)
            next(norms)
            splits(2)
            next(soft)
            next(norms)
            splits(2)
            next(soft)
            for _ in norms:
                pass
            probT_copies(MOBA_GROUPS, 1)
            y_lo(4, lambda n: (yT_lo[:, 4 * (n % 2):4 * (n % 2) + 4, (n // 2) * P:(n // 2 + 1) * P],
                               bank[:, 4 + n, :].rearrange("p (i q) -> p i q", i=4),
                               yT_hi[:, 4 * (n % 2):4 * (n % 2) + 4, (n // 2) * P:(n // 2 + 1) * P]))
            v = v_next[0] - LEAD
            splits(8)
            add_residual(1.0, v + 8)
            cross(1, False)
            norm(COL_OF["ffn2"] + KD, xT_hi, xT_lo)
            ffn()
            dve.wait_ge(sem["gain_loaded"], 16)
            rstd_of_both()
            for t in range(NT):
                dve.scalar_tensor_tensor(x[:, t, :], x[:, t, :], rstd[:, t:t + 1], gain_row[:, :],
                                         ALU.mult, ALU.mult).then_inc(sem["residual"], 1)
            norm(COL_OF["ffn1_2"], xT_hi, xT_lo)
            ffn()
            norm(COL_OF["mix_2"], xT_hi, xT_lo)
            splits(2)
            link(dve.memset(glu[:, :, 0:PAD], 0.0))
            dve.wait_ge(sem["gla_const"], N_GLA_CONST)
            c.next("rank_psum")
            for i in range(2):
                g = COL_OF["gate_b_2"] + i
                link(dve.tensor_scalar(g_z[:, i * T:(i + 1) * T], bank[:, 7, i * T:(i + 1) * T], cols[:, g:g + 1],
                                       None, ALU.add))
            link(dve.scalar_tensor_tensor(g_l, g_z, -1.0, g_z, ALU.mult, ALU.min), "decays")
            splits(2)
            c.next("act_step", 2)
            link(dve.scalar_tensor_tensor(g_z, g_z, 0.0, g_l, ALU.min, ALU.subtract))
            dve.tensor_tensor_scan(g_cum[:, 0:T], reset, g_z[:, 0:T], 0.0, ALU.mult, ALU.add)
            link(dve.tensor_tensor_scan(g_cum[:, T:2 * T], reset, g_z[:, T:2 * T], 0.0, ALU.mult, ALU.add), "decays")
            chunks = g_cum.rearrange("p (n c) -> p n c", c=64)
            link(dve.tensor_copy(decay_in, chunks[:, :, 63]))
            link(dve.tensor_tensor(e_end.rearrange("p (n c) -> p n c", c=64), decay_in[:, :, None].to_broadcast([P, 8, 64]),
                                   chunks, ALU.subtract), "decays")
            splits(2)
            P1 = PROJ_BEFORE_2
            dve.wait_ge(sem["proj_sb"], P1 + 3)
            c.next("act_step")
            dve.scalar_tensor_tensor(q_dec, g_q, 0.125, e_pos, ALU.mult, ALU.mult)
            dve.tensor_tensor(k_neg, g_k, e_neg, ALU.mult).then_inc(sem["gla_operands"], 1)
            dve.scalar_tensor_tensor(q_neg, g_q, 0.125, e_neg, ALU.mult, ALU.mult)
            dve.tensor_tensor(k_pos, g_k, e_pos, ALU.mult).then_inc(sem["gla_operands"], 1)
            c.next("act_step")
            dve.tensor_tensor(k_end, g_k, e_end, ALU.mult).then_inc(sem["gla_operands"], 1)
            splits(8)
            for n in range(2):
                dve.wait_ge(sem["proj_sb"], P1 + 5 + 2 * n)
                s = slice(2 * n, 2 * n + 2)
                link(dve.tensor_tensor(glu[:, s, PAD:PAD + T], glu[:, s, PAD:PAD + T], sig_b[:, s, :], ALU.mult))
            w = COL_OF["conv_w_2"]
            for n in range(4):
                b = COL_OF["conv_b_2"] + n
                dve.tensor_scalar(conv_acc[:, n, :], glu[:, n, 0:T], cols[:, w + n:w + n + 1], cols[:, b:b + 1],
                                  ALU.mult, ALU.add).then_inc(sem["conv_tap"], 1)

            def taps(lo, hi):
                with dve.Fori(lo, hi) as j:
                    for n in range(4):
                        dve.wait_ge(sem["conv_tap"], 4 * j + n - 3)
                        dve.scalar_tensor_tensor(conv_acc[:, n, :], glu[:, n, bass.ds(j, T)],
                                                 cols[:, bass.ds(4 * j + w + n, 1)], conv_acc[:, n, :],
                                                 ALU.mult, ALU.add).then_inc(sem["conv_tap"], 1)

            for n in range(8):
                taps(1 + 3 * n, 4 + 3 * n)
                split()
            taps(25, CONV_TAPS)
            c.skip("conv_tap", 4 * CONV_TAPS)
            c.next("mean_psum")
            dve.tensor_tensor(centred[:, :, :], conv_acc[:, :, :], bank[:, 5, None, 0:T].to_broadcast([P, 4, T]),
                              ALU.subtract).then_inc(sem["var_in"], 1)
            c.next("gla_scores", 2)
            for m, b in ((low_mask, 0), (up_mask, 2)):
                for h in range(2):
                    dst = score[:, h, :].rearrange("p (n t) -> p n t", n=4)
                    mask = m.bitcast(U32)[:, None, :].to_broadcast([P, 4, P])
                    link(dve.copy_predicated(dst, mask, bank[:, b + h, :].rearrange("p (n t) -> p n t", n=4)),
                         "score_ready")
            c.next("kv_psum")
            link(dve.tensor_copy(state[:, 0, :], bank[:, 6, 0:T]))
            for i in range(2):
                s = slice(i * P, (i + 1) * P)
                link(dve.scalar_tensor_tensor(state[:, 1, s], state[:, 0, s], decay[:, 4 * i + 1:4 * i + 2],
                                              bank[:, 7, s], ALU.mult, ALU.add))
            for i in range(2):
                s = slice(i * P, (i + 1) * P)
                last = dve.scalar_tensor_tensor(state[:, 2, s], state[:, 1, s], decay[:, 4 * i + 2:4 * i + 3],
                                                bank[:, 6, T + i * P:T + (i + 1) * P], ALU.mult, ALU.add)
            last.then_inc(sem["states_ready"], 1)
            dve.wait_ge(sem["gla_gain_loaded"], 16)
            dve.wait_ge(sem["proj_sb"], P1 + 11)
            link(dve.tensor_tensor(g_r[:, :, :], g_r[:, :, :], gla_gain[:, None, :].to_broadcast([P, NT, 512]), ALU.mult))
            c.next("var_psum")
            link(dve.tensor_copy(k_end[:, 0:T], bank[:, 5, T:2 * T]))
            rsqrt(ln_rstd, k_end[:, 0:T], k_end[:, T:2 * T])
            dve.tensor_tensor(centred[:, :, :], centred[:, :, :], ln_rstd[:, None, :].to_broadcast([P, 4, T]), ALU.mult)\
                .then_inc(sem["ln_ready"], 1)
            c.next("o_square", 2)
            for h in range(2):
                link(dve.tensor_reduce(o_ms[:, 4 * h:4 * h + 4], score[:, h, :].rearrange("p (n t) -> p n t", n=4),
                                       AX.X, ALU.add))
            link(dve.tensor_scalar(o_ms, o_ms, 1.0 / P, None, ALU.mult))
            rsqrt(o_rstd, o_ms, small[:, 200:208])
            for h in range(2):
                o = o_nat.rearrange("p t (i h d) -> p h t i d", i=2, h=2)[:, h]
                r = g_r.rearrange("p t (i h d) -> p h t i d", i=2, h=2)[:, h]
                src = bank[:, h, :].rearrange("p (t i d) -> p t i d", t=2, i=2)
                rs = o_rstd[:, 4 * h:4 * h + 4].rearrange("p (t i) -> p t i", t=2)[:, :, :, None]
                link(dve.tensor_tensor(o, src, rs.to_broadcast([P, 2, 2, P]), ALU.mult))
                dve.tensor_tensor(o, o, r, ALU.mult).then_inc(sem["gated"], 1)
            y_lo(3, lambda n: (yT_lo[:, 0:4, :], conv_acc[:, :, :], yT_hi[:, 0:4, :]) if n == 0 else
                 (yT_lo[:, 2 + 2 * n:4 + 2 * n, :], halves(bank[:, 1 + n, :]), yT_hi[:, 2 + 2 * n:4 + 2 * n, :]))
            v = v_next[0] - LEAD
            splits(8)
            add_residual(1.0, v + 8)
            norm(COL_OF["ffn2_2"], xT_hi, xT_lo)
            ffn()
            norm(COL_OF["ple_2"], xT_hi, xT_lo)
            y_lo(1, lambda n: (yT_lo[:, 0:2, :], halves(bank[:, 0, :]), yT_hi[:, 0:2, :]))
            splits(10)
            for t in range(NT):
                dve.wait_ge(sem["proj_sb"], P1 + 11 + 2 + t + 1)
                link(dve.tensor_tensor(ple_gate[:, t, :], ple_gate[:, t, :], p_out[:, t, :], ALU.mult))
                dve.tensor_tensor(x[:, t, :], x[:, t, :], ple_gate[:, t, :], ALU.add).then_inc(sem["residual"], 1)
            dve.wait_ge(sem["gain_loaded"], 32)
            rstd_of_both()
            for t in range(NT):
                dve.scalar_tensor_tensor(xn[:, t, :], x[:, t, :], rstd[:, t:t + 1], gain_row[:, :],
                                         ALU.mult, ALU.mult).then_inc(sem["result_ready"], 1)

        @block.tensor
        def _(pe):
            c = Counter(pe, sem)
            v_next = [0]

            def split_ready(v, i):
                pe.wait_ge(sem["lo_ready"], v + 1 if i is None else v + 1 + LOOP_HALVES * i)

            def products(dst, lhs, rhs, start, stop):
                for n, (l, r) in enumerate(((0, 0), (0, 1), (1, 0))):
                    last = pe.matmul(dst, lhs[l], rhs[r], start=start and n == 0, stop=stop and n == 2)
                return last

            def w_cols(v, k, n=P):
                return tuple(m[:, v % SPL, k * n:(k + 1) * n] for m in (w_hi, w_lo))

            def xk(xs, k):
                return tuple(m[:, k, :] for m in xs)

            X, Y, MEM, HID = (xT_hi, xT_lo), (yT_hi, yT_lo), (memT_hi, memT_lo), (hid_hi, hid_lo)

            def transposed(v, dst, xs, i=None, first=False):
                split_ready(v, i)
                for k in range(KD):
                    if first and k % 2 == 0:
                        c.next("xT_lo_ready")
                    last = products(dst, w_cols(v, k), xk(xs, k), k == 0, k == KD - 1)
                last.then_inc(sem["half_done"], 1)

            def natural(v, dst, xs, first=False):
                split_ready(v, None)
                for t in range(NT):
                    for k in range(KD):
                        last = products(dst[:, t, :], tuple(m[:, k, t * P:(t + 1) * P] for m in xs), w_cols(v, k),
                                        k == 0, k == KD - 1)
                last.then_inc(sem["half_done"], 1)

            def take():
                v_next[0] += 1
                return v_next[0] - 1

            def col_unit(b, xs, first=False):
                for f in range(2):
                    transposed(take(), bank[:, b, f * T:(f + 1) * T], xs, first=first and f == 0)

            def nat_unit(b, xs):
                dst = bank[:, b, :].rearrange("p (t f) -> p t f", t=NT)
                for f in range(2):
                    natural(take(), dst[:, :, f * P:(f + 1) * P], xs)

            def row_half(v, out_of, ys, tile, start, stop, i=None, signal=False):
                split_ready(v, i)
                for t in range(NT):
                    for n in range(2):
                        last = products(out_of(t, n), tuple(m[:, tile, t * P:(t + 1) * P] for m in ys),
                                        w_cols(v, n, 512), start, stop)
                    if signal and t == 0:
                        last.then_inc(sem["acc_ready"], 1)
                last.then_inc(sem["half_done"], 1)

            def row_units(n_tiles, ys, out_of=d_bank, signal=True, first=False):
                for tile in range(n_tiles):
                    if first and tile % 2 == 0:
                        c.next("xT_lo_ready")
                    row_half(take(), out_of, ys, tile, tile == 0, tile == n_tiles - 1,
                             signal=signal and tile == n_tiles - 1)

            def norm():
                for t in range(NT):
                    c.next("normed")
                    for k in range(KD):
                        at = (k % 2) * T + t * P
                        last = pe.transpose(bank[:, k // 2, at:at + P], xn[:, t, k * P:(k + 1) * P], ident[:, :])
                        if t == 1 and k % 2:
                            last.then_inc(sem["xT_psum"], 1)

            n_ffn = [0]

            def ffn():
                v0, j0 = 2 * ffns[n_ffn[0]][0], NJ * n_ffn[0]
                n_ffn[0] += 1
                assert v_next[0] == v0

                def gate_up(j, i=None):
                    v = v0 + (4 + 6 * (j - 1) if j else 0)
                    for n in range(4):
                        dst = bank[:, 2 * (j % 2) + n // 2, (n % 2) * T:(n % 2 + 1) * T]
                        transposed(v + n, dst, X, i, first=j == 0 and n == 0)

                def down(j, v, i=None, signal=False):
                    ready = j0 + j + 1
                    pe.wait_ge(sem["hidden_lo_ready"], ready if i is None else ready + 2 * i)
                    for s in range(2):
                        row_half(v + s, d_bank, HID, 2 * (j % 2) + s, j == 0 and s == 0, j == NJ - 1 and s == 1, i,
                                 signal and s == 1)

                gate_up(0)
                gate_up(1)
                down(0, v0 + 8)
                with pe.Fori(0, LOOPS) as i:
                    for j in (2, 3):
                        gate_up(j, i)
                        down(j - 1, v0 + 6 * j + 2, i)
                gate_up(NJ - 1)
                down(NJ - 2, v0 + 6 * (NJ - 1) + 2)
                down(NJ - 1, v0 + FFN_HALVES - 2, signal=True)
                v_next[0] = v0 + FFN_HALVES

            def score_groups(groups, q_of, k_of):
                for g, (t, heads, nk) in enumerate(groups):
                    for n, h in enumerate(heads):
                        last = pe.matmul(bank[:, g, n * nk:(n + 1) * nk], q_of(h, t), k_of(h, nk), start=True, stop=True)
                    last.then_inc(sem["scores"], 1)

            def transpose_probs(groups):
                for g, (t, heads, nk) in enumerate(groups):
                    c.next("probs_ready")
                    for blk in range(4):
                        last = pe.transpose(bank[:, (len(groups) + g) % 8, blk * P:(blk + 1) * P],
                                            prob[:, g, blk * P:(blk + 1) * P], ident[:, :])
                    last.then_inc(sem["probT_psum"], 1)

            def values(groups, v_of, out_of, last_head):
                for g, (t, heads, nk) in enumerate(groups):
                    c.next("probT_odd" if g % 2 else "probT_even")
                    for n, h in enumerate(heads):
                        for kb in range(nk // P):
                            blk = n * (nk // P) + kb
                            last = pe.matmul(out_of(h, t), v_of(h, kb), probT[:, g, blk * P:(blk + 1) * P],
                                             start=kb == 0, stop=kb == nk // P - 1)
                        if h in last_head:
                            last.then_inc(sem["out_psum"], 1)

            pe.wait_ge(sem["pool_const"], 5)
            pe.wait_ge(sem["vectors_loaded"], 16 * 15)
            pe.transpose(bank[:, 7, 0:P], col_rows[:, 0, :], ident[:, :])
            n = N_COLS - P
            pe.transpose(bank[:, 7, P:N_COLS], col_rows[0:n, 1, :], ident[0:n, 0:n]).then_inc(sem["vectors_psum"], 1)
            norm()
            c.next("xT_lo_ready", 4)
            norm()
            ffn()
            pe.wait_ge(sem["bias_rev_loaded"], 16)
            for n in range(4):
                rev = bias_rev[:, 2 * n:2 * n + 2, :]
                pe.matmul(bank[:, n, :], flip, rev, start=True, stop=True).then_inc(sem["bias_psum"], 1)
            c.next("bias_ready", 4)
            norm()
            col_unit(0, X, first=True)
            col_unit(1, X)
            v = take()
            transposed(v, bank[:, 2, 0:T], X)
            natural(take(), bank[:, 2, T:2 * T].rearrange("p (t f) -> p t f", t=NT), X)
            col_unit(6, X)
            col_unit(7, X)
            c.next("proj_sb", 3)
            score_groups(SWA_GROUPS,
                         lambda h, t: q_sb[64 * (h // 4):64 * (h // 4) + 64, h % 4, t * P:(t + 1) * P],
                         lambda h, nk: swa_k[64 * (h // 4):64 * (h // 4) + 64, 0:nk])
            for b in (6, 7, 6, 7):
                c.next("proj_sb")
                col_unit(b, X)
            c.next("proj_sb", 2)
            transpose_probs(SWA_GROUPS)
            values(SWA_GROUPS, lambda h, kb: swa_v[:, kb, 64 * (h // 4):64 * (h // 4) + 64],
                   lambda h, t: bank[64 * (h % 2):64 * (h % 2) + 64, 4 + t, (h // 2) * P:(h // 2 + 1) * P], (7,))
            c.next("y_lo_ready", 4)
            row_units(8, Y)

            def cross(kv):
                norm()
                col_unit(0, X, first=True)
                col_unit(1, X)
                if kv:
                    for b in (2, 3):
                        col_unit(b, MEM)
                    for b in (4, 5):
                        nat_unit(b, MEM)
                c.next("proj_sb", 6 if kv else 2)
                score_groups(XA_GROUPS, lambda h, t: q_sb[:, h, t * P:(t + 1) * P], lambda h, nk: mem_k[:, h, :])
                transpose_probs(XA_GROUPS)
                values(XA_GROUPS, lambda h, kb: mem_v[:, kb, h * P:(h + 1) * P],
                       lambda h, t: bank[:, t, h * P:(h + 1) * P], (3,))
                c.next("y_lo_ready", 2)
                row_units(4, Y)

            cross(True)
            norm()
            ffn()
            norm()
            ffn()
            norm()
            for b in range(6):
                col_unit(b, X, first=b == 0)
            for b in (6, 7):
                nat_unit(b, X)
            c.next("proj_sb", 8)
            score_groups(MOBA_GROUPS, lambda h, t: q_sb[:, h, t * P:(t + 1) * P], lambda h, nk: k_sb[:, h // 2, 0:nk])
            for n, b in enumerate((6, 7, 6, 7)):
                if n >= 2:
                    c.next("proj_sb")
                (col_unit if n < 2 else nat_unit)(b, MEM)
            c.next("proj_sb", 2)
            transpose_probs(MOBA_GROUPS)
            values(MOBA_GROUPS, lambda h, kb: v_sb[:, kb, (h // 2) * P:(h // 2 + 1) * P],
                   lambda h, t: bank[:, 4 + 2 * t + h // 4, (h % 4) * P:(h % 4 + 1) * P], (3, 7))
            c.next("y_lo_ready", 4)
            row_units(8, Y)
            cross(False)
            norm()
            ffn()
            norm()
            ffn()
            norm()
            for half in range(2):
                v = take()
                split_ready(v, None)
                for k in range(4 * half, 4 * half + 4):
                    if k % 2 == 0:
                        c.next("xT_lo_ready")
                    last = products(bank[:, 0, 0:T], w_cols(v, k % 4), xk(X, k), k == 0, k == KD - 1)
                last.then_inc(sem["half_done"], 1)
            col_unit(5, X)
            c.next("proj_sb")
            pe.wait_ge(sem["rank_loaded"], 16)
            for i in range(2):
                last = pe.matmul(bank[:, 7, i * T:(i + 1) * T], rank_w[:, i * P:(i + 1) * P], rank_x[:, :],
                                 start=True, stop=True)
            last.then_inc(sem["rank_psum"], 1)
            col_unit(6, X)
            for b in (1, 2, 3, 4):
                col_unit(b, X)
            c.next("decays")
            nat_unit(7, X)
            nat_unit(0, X)
            c.next("proj_sb", 4)
            nat_unit(1, X)
            nat_unit(2, X)
            c.next("proj_sb", 6)

            def tile_at(m, i, tt, h):
                return m[64 * h:64 * h + 64, i * T + tt * P:i * T + (tt + 1) * P]

            for b, (k, q) in ((0, (k_neg, q_dec)), (2, (k_pos, q_neg))):
                c.next("gla_operands")
                for h in range(2):
                    for tt in range(NT):
                        for i in range(2):
                            at = (2 * tt + i) * P
                            last = pe.matmul(bank[:, b + h, at:at + P], tile_at(k, i, tt, h), tile_at(q, i, tt, h),
                                             start=True, stop=True)
                last.then_inc(sem["gla_scores"], 1)
            c.next("gla_operands")
            for tt in range(NT):
                for i in range(2):
                    last = pe.transpose(bank[:, 4, (2 * tt + i) * P:(2 * tt + i + 1) * P],
                                        k_end[:, i * T + tt * P:i * T + (tt + 1) * P], ident[:, :])
            last.then_inc(sem["k_nat_psum"], 1)
            c.next("k_nat_ready")
            for ch in (0, 2, 1):
                tt, r = ch // 2, ch % 2
                for h in range(2):
                    for i in range(2):
                        head = 2 * i + h
                        at = (2 * tt + i) * P if r == 0 else i * P
                        last = pe.matmul(bank[64 * h:64 * h + 64, 6 + r, at:at + P],
                                         k_nat[64 * r:64 * r + 64, (2 * tt + i) * P + 64 * h:(2 * tt + i) * P + 64 * h + 64],
                                         g_v[64 * r:64 * r + 64, tt, head * P:(head + 1) * P], start=True, stop=True)
            last.then_inc(sem["kv_psum"], 1)
            pe.wait_ge(sem["conv_tap"], 4 * CONV_TAPS)
            for n in range(4):
                last = pe.matmul(bank[:, 5, 0:T], ones, conv_acc[:, n, :], start=n == 0, stop=n == 3)
            last.then_inc(sem["mean_psum"], 1)
            c.next("var_in", 2)
            for n in range(4):
                last = pe.matmul(bank[:, 5, T:2 * T], ones, sq_c[:, n, :], start=n == 0, stop=n == 3)
            last.then_inc(sem["var_psum"], 1)
            c.next("score_ready", 4)
            c.next("states_ready")
            for h in range(2):
                for tt in range(NT):
                    for i in range(2):
                        head, at = 2 * i + h, (2 * tt + i) * P
                        pe.matmul(bank[:, h, at:at + P], score[:, h, at:at + P], g_v[:, tt, head * P:(head + 1) * P],
                                  start=True, stop=False, skip_group_check=True)
                        for ch in (1,) if tt == 0 else (2, 3):
                            r = ch % 2
                            last = pe.matmul(bank[64 * r:64 * r + 64, h, at:at + P],
                                             q_dec[64 * h:64 * h + 64, i * T + ch * 64:i * T + ch * 64 + 64],
                                             state[64 * h:64 * h + 64, ch - 1, i * P:(i + 1) * P],
                                             start=False, stop=True, skip_group_check=True)
            last.then_inc(sem["out_psum"], 1)
            c.next("gated", 2)
            for head in range(4):
                for tt in range(NT):
                    at = (head % 2) * T + tt * P
                    last = pe.transpose(bank[:, 2 + head // 2, at:at + P], o_nat[:, tt, head * P:(head + 1) * P],
                                        ident[:, :])
                if head % 2:
                    last.then_inc(sem["out_psum"], 1)
            c.next("y_lo_ready", 3)
            row_units(8, Y)
            norm()
            ffn()
            norm()
            c.next("xT_lo_ready", 4)
            pe.wait_ge(sem["p_loaded"], 16)
            for k in range(2):
                for t in range(NT):
                    last = pe.transpose(bank[:, 0, k * T + t * P:k * T + (t + 1) * P], p_in[:, t, k * P:(k + 1) * P],
                                        ident[:, :])
            last.then_inc(sem["out_psum"], 1)
            c.next("y_lo_ready")
            row_units(2, Y, out_of=lambda t, n: bank[:, 2 * t + n, :], signal=False)
            row_units(8, X, signal=False)
            assert v_next[0] == n_half


def kernel(**inputs):
    import concourse.bacc as bacc
    from concourse.bass_utils import run_bass_kernel_spmd

    nc = bacc.Bacc("TRN2", target_bir_lowering=False, num_devices=1)
    arrays, aps = {}, {}
    for name, value in inputs.items():
        array = np.ascontiguousarray(value)
        arrays[f"in_{name}"] = array
        aps[name] = nc.dram_tensor(f"in_{name}", array.shape, mybir.dt.from_np(array.dtype), kind="ExternalInput").ap()
    out = nc.dram_tensor("result", (1, T, D), F32, kind="ExternalOutput").ap()
    build(nc, aps, out)
    r = run_bass_kernel_spmd(nc, [arrays], core_ids=[0])
    return r.results[0]["result"]
```

```python
from contextlib import ExitStack

import numpy as np

import concourse.bass as bass
from concourse import mybir

P = 128
T = 256
NT = T // P
D = 1024
KD = D // P
FF = 2816
UC = 256
NJ = FF // UC
HALF = 1024
SWA_GROUPS = [(0, [0, 1, 2, 3], 128), (0, [4, 5, 6, 7], 128)] + [(1, [h, h + 1], 256) for h in (0, 2, 4, 6)]
MOBA_GROUPS = SWA_GROUPS
XA_GROUPS = [(t, [h, h + 1], 256) for t in range(2) for h in (0, 2)]
PROJ_BEFORE_2 = 3 + 2 + 6 + 2
NAT_BEFORE_2 = 7 + 4 + 2 + 4
ACC_BEFORE_PLE = 3 * 11
RAW = 3
SPL = 6
LEAD = SPL - 1
EPS = 1e-6
MASKED = -1e38
ROWS, COLS, PAIRED, RANK = "rows", "cols", "paired", "rank"
GATE_RANK = 16
CONV_TAPS = 31
DVE_TILES = 2

F32 = mybir.dt.float32
F32R = mybir.dt.float32r
U32 = mybir.dt.uint32
ALU = mybir.AluOpType
ACT = mybir.ActivationFunctionType
AX = mybir.AxisListType

VECTORS, COL_OF, _at = [], {}, 0
for _input, _name, _n in (("ffn1_norm", "ffn1", 16), ("mix_norm", "mix", 16), ("xa_norm", "xa", 16),
                          ("ffn2_norm", "ffn2", 16), ("mem_norm", "mem", 8), ("ffn1_norm_2", "ffn1_2", 8),
                          ("mix_norm_2", "mix_2", 8), ("ffn2_norm_2", "ffn2_2", 8), ("ple_norm_2", "ple_2", 8),
                          ("ev_conv_w", "conv_w", 12), ("conv_b_2", "conv_b_2", 4), ("conv_ln_g_2", "ln_g_2", 4),
                          ("conv_ln_b_2", "ln_b_2", 4), ("conv_w_2", "conv_w_2", 124), ("gate_b_2", "gate_b_2", 2)):
    VECTORS.append((_input, _n, _at))
    COL_OF[_name] = _at
    _at += _n
N_COLS = _at


def bucket_starts():
    d = np.arange(256)
    nf = np.maximum(d, 1).astype(np.float32)
    large = 16 + (np.log(nf / np.float32(16)) / np.float32(np.log(8.0)) * np.float32(16)).astype(np.int32)
    b = np.where(d < 16, d, np.minimum(large, 31))
    return [int(np.argmax(b == n)) for n in range(32)] + [256]


def rows_of_vector(ap):
    dims = "abc"[:len(ap.shape)]
    flat = ap.rearrange(f"{' '.join(dims)} -> ({' '.join(dims)})") if len(dims) > 1 else ap
    return flat.rearrange("(r c) -> r c", c=P)


class Counter:

    def __init__(self, eng, sems):
        self.eng, self.sems, self.seen = eng, sems, {n: 0 for n in sems}

    def next(self, name, n=1):
        self.seen[name] += n
        self.eng.wait_ge(self.sems[name], self.seen[name])

    def skip(self, name, n):
        self.seen[name] += n


def build(nc, a, out):

    units = []

    def col_unit(w, c0):
        units.append((COLS, w.rearrange("(k p) f -> p k f", p=P)[:, :, c0:c0 + UC]))

    def row_unit(w, r0):
        units.append((ROWS, w[r0:r0 + UC, :].rearrange("(s p) n -> p s n", p=P)))

    def ffn_units(gate, up, down):
        col_unit(gate, 0)
        col_unit(up, 0)
        for j in range(1, NJ):
            col_unit(gate, j * UC)
            col_unit(up, j * UC)
            row_unit(down, (j - 1) * UC)
        row_unit(down, (NJ - 1) * UC)

    ffns = []

    def ffn(gate, up, down):
        ffns.append((len(units), gate, up, down))
        ffn_units(gate, up, down)

    def cols_of(w, c0, n):
        for c in range(c0, c0 + n, UC):
            col_unit(w, c)

    def rows_of(w):
        for r in range(0, w.shape[0], UC):
            row_unit(w, r)

    for l in range(2):
        ffn(a["ffn1_w_gate"][l], a["ffn1_w_up"][l], a["ffn1_w_down"][l])
        if l == 0:
            w = a["ev_w_in"][0]
            pairs = w[:, 1536:2048].rearrange("(k p) (h c) -> p k h c", p=P, h=2)
            for i in range(2):
                units.append((PAIRED, pairs[:, :, :, i * P:(i + 1) * P]))
            col_unit(w, 2048)
            for c in (512, 1024, 768, 1280, 0, 256):
                col_unit(w, c)
            for r in (512, 768, 0, 256):
                row_unit(a["ev_w_out"][0], r)
            cols_of(a["xa_w_q"][l], 0, 512)
            cols_of(a["xa_w_kv"][l], 0, 1024)
        else:
            cols_of(a["od_w_in"][0], 0, 2048)
            cols_of(a["xa_w_kv"][l], 0, 1024)
            rows_of(a["od_w_out"][0])
            cols_of(a["xa_w_q"][l], 0, 512)
        rows_of(a["xa_w_o"][l])
        ffn(a["ffn2_w_gate"][l], a["ffn2_w_up"][l], a["ffn2_w_down"][l])
    w = a["ffn1_w_in_2"][0]
    ffn(w[:, 0:FF], w[:, FF:2 * FF], a["ffn1_w_out_2"][0])
    w = a["w_in_2"][0]
    units.append((RANK, w.rearrange("(k p) f -> p k f", p=P)[:, :, w.shape[1] - P:w.shape[1]]))
    for c in (1024, 1280, 0, 512, 256, 768, 1536, 1792, 2048, 2304):
        col_unit(w, c)
    for r in (512, 768, 0, 256):
        row_unit(a["w_out_2"][0], r)
    w = a["ffn2_w_in_2"][0]
    ffn(w[:, 0:FF], w[:, FF:2 * FF], a["ffn2_w_out_2"][0])
    rows_of(a["ple_w_proj_2"][0])
    rows_of(a["ple_w_gate_2"][0])
    n_half = 2 * len(units)
    landed, in_slot = [], [0] * RAW
    for u, (kind, _) in enumerate(units):
        in_slot[u % RAW] += 32 if kind == PAIRED else 16
        landed.append(in_slot[u % RAW])

    with ExitStack() as ctx:
        def sb(name, shape, dt=F32):
            return ctx.enter_context(nc.sbuf_tensor(name, shape, dt))

        raw = sb("raw", [P, RAW, 2 * HALF])
        w_hi = sb("w_hi", [P, SPL, HALF], F32R)
        w_lo = sb("w_lo", [P, SPL, HALF], F32R)
        x = sb("x", [P, NT, D])
        xT_hi = sb("xT_hi", [P, KD, T], F32R)
        xT_lo = sb("xT_lo", [P, KD, T], F32R)
        yT_hi = sb("yT_hi", [P, KD, T], F32R)
        yT_lo = sb("yT_lo", [P, KD, T], F32R)
        memT_hi = sb("memT_hi", [P, KD, T], F32R)
        memT_lo = sb("memT_lo", [P, KD, T], F32R)
        hid_hi = sb("hid_hi", [P, 4, T], F32R)
        hid_lo = sb("hid_lo", [P, 4, T], F32R)
        arena = sb("arena", [P, 12288])
        bias = sb("bias", [P, 8, T])
        gain_row = sb("gain_row", [P, D])
        cols = sb("cols", [P, 256])
        ident = sb("ident", [P, P])
        unit_sq = sb("unit_sq", [P, P])
        diag = sb("diag", [P, NT, P])
        scale_row = sb("scale_row", [P, T])
        small = sb("small", [P, 256])
        rank_w = sb("rank_w", [P, T])
        rank_x = sb("rank_x", [P, T])
        table = sb("table", [8, 32])
        spread = sb("spread", [8, 384])
        bank = ctx.enter_context(nc.psum_tensor("bank", [P, 8, 512], F32))

        mean_sq, rstd = small[:, 0:2], small[:, 2:4]
        both_gains = small[:, 212:220]
        first_rstd = small[:, 228:230]
        mem_sq, mem_rstd = small[:, 208:210], small[:, 210:212]
        sink, neg_sink = small[:, 8:16], small[:, 16:24]
        neg_max, top = small[:, 24:48], small[:, 48:72]
        den, inv = small[:, 72:96], small[:, 96:120]
        sink_in, sink_e = small[:, 120:144], small[:, 144:168]
        decay_in = small[:, 168:176]
        decay = small[:, 176:184]
        o_ms, o_rstd = small[:, 184:192], small[:, 192:200]

        mem_in = arena[:, 8192:10240].rearrange("p (t d) -> p t d", t=NT)
        junk = arena[:, 0:1024]
        result = arena[:, 0:2048].rearrange("p (t d) -> p t d", t=NT)
        prob = arena[:, 0:3072].rearrange("p (g c) -> p g c", c=512)
        probT = arena[:, 3072:6144].rearrange("p (g c) -> p g c", c=512)
        act_gate = arena[:, 3072:4096].rearrange("p (j c) -> p j c", j=2)
        hidden = arena[:, 4096:5120].rearrange("p (j c) -> p j c", j=2)
        q_sb = arena[:, 6144:8192].rearrange("p (h t) -> p h t", t=T)
        k_sb = arena[:, 8192:9216].rearrange("p (h t) -> p h t", t=T)
        v_sb = arena[:, 9216:10240].rearrange("p (t d) -> p t d", t=NT)
        mem_k = arena[:, 10240:11264].rearrange("p (h t) -> p h t", t=T)
        mem_v = arena[:, 11264:12288].rearrange("p (t d) -> p t d", t=NT)
        bias_rev = arena[:, 10240:12288].rearrange("p (h c) -> p h c", h=8)
        flip = arena[:, 2048:2176]
        col_rows = arena[:, 2176:2432].rearrange("p (a c) -> p a c", a=2)
        swa_k, swa_v = k_sb[:, 0, :], arena[:, 9216:9472].rearrange("p (t d) -> p t d", t=NT)
        conv_c = arena[:, 7168:8192].rearrange("p (n c) -> p n c", n=2)
        conv_u = arena[:, 8448:8960]
        conv_v = arena[:, 9472:9988].rearrange("p (n c) -> p n c", n=2)
        conv_b = arena[:, 10240:11264].rearrange("p (n c) -> p n c", n=2)
        conv_y = arena[:, 11264:12288].rearrange("p (n c) -> p n c", n=2)
        PAD = CONV_TAPS - 1
        glu = arena[:, 0:4 * (T + PAD)].rearrange("p (n c) -> p n c", n=4)
        conv_acc = arena[:, 1152:2176].rearrange("p (n c) -> p n c", n=4)
        sig_b = arena[:, 2176:3200].rearrange("p (n c) -> p n c", n=4)
        centred = arena[:, 2176:3200].rearrange("p (n c) -> p n c", n=4)
        g_q, g_k = arena[:, 3200:3712], arena[:, 3712:4224]
        g_v = arena[:, 4224:5248].rearrange("p (t d) -> p t d", t=NT)
        g_r = arena[:, 5248:6272].rearrange("p (t d) -> p t d", t=NT)
        g_z, g_l, g_cum = arena[:, 6272:6784], arena[:, 6784:7296], arena[:, 7296:7808]
        e_pos, e_neg, e_end = arena[:, 7808:8320], arena[:, 8320:8832], arena[:, 8832:9344]
        q_dec, q_neg = g_z, g_l
        k_neg, k_pos, k_end = arena[:, 9344:9856], arena[:, 9856:10368], arena[:, 10368:10880]
        k_nat = e_pos
        score = arena[:, 10880:11904].rearrange("p (h c) -> p h c", h=2)
        ones = arena[:, 11904:12032]
        ln_rstd = e_end[:, 0:T]
        low_mask, up_mask = arena[:, 12032:12160], arena[:, 12160:12288]
        state = bias[:, 0:3, :]
        reset = bias[:, 3, :]
        gla_gain = bias[:, 4:6, :].rearrange("p a c -> p (a c)")
        sq_c = arena[:, 0:1024].rearrange("p (n c) -> p n c", n=4)
        o_nat = arena[:, 9344:10368].rearrange("p (t d) -> p t d", t=NT)
        p_in = arena[:, 6144:6656].rearrange("p (t c) -> p t c", t=NT)
        p_out = arena[:, 7168:9216].rearrange("p (t d) -> p t d", t=NT)
        ple_gate = arena[:, 9216:11264].rearrange("p (t d) -> p t d", t=NT)


        def tap_diag(tile, j):
            hi, lo = (memT_hi, memT_lo) if tile == 2 else (yT_hi, yT_lo)
            m, j = (lo, j - 16) if j >= 16 else (hi, j)
            return m[:, :, :].rearrange("p k t -> p (k t)").bitcast(F32)[:, j * P:(j + 1) * P]

        spread_dram = nc.dram_tensor("spread_dram", [8, 384], F32).ap()
        bias_dram = nc.dram_tensor("bias_dram", [P, 8 * T], F32).ap()

        names = """vectors_loaded first_gains_loaded first_gains_psum x_loaded mem_loaded table_loaded sinks_loaded gain_loaded rank_loaded
            p_loaded gla_gain_loaded spread_stored bias_rev_loaded bias_stored bias_loaded out_stored
            pool_const spread_ready bias_masked gla_const rank_zero tap_diags
            vectors_psum cols_ready bias_psum bias_ready
            hi_ready lo_ready half_done
            residual mean_sq mem_normed diag_ready scale_psum scale_ready scaled xT_psum xT_hi_ready xT_lo_ready acc_ready
            gate_scaled up_scaled act_gate_ready hidden_ready hidden_hi_ready hidden_lo_ready
            proj_sb nat_sb scores max_ready exp_ready probs_ready probT_psum probT_even probT_odd
            out_psum y_hi_ready y_lo_ready conv_v_ready conv_ready conv_tap dve_step act_step
            rank_psum decays gla_operands gla_scores score_ready kv_psum states_ready ln_ready
            k_nat_psum k_nat_ready glu_ready conv_psum conv_evac o_square gated mean_psum var_in var_psum result_ready""".split()
        sem = {n: ctx.enter_context(nc.semaphore(n)) for n in names}
        raw_ready = [ctx.enter_context(nc.semaphore(f"raw_ready{i}")) for i in range(RAW)]
        block = ctx.enter_context(nc.Block())

        def d_bank(t, n):
            return bank[:, 4 + 2 * t + n, :]

        def raw_half(v):
            kind = units[v // 2][0]
            slot = raw[:, (v // 2) % RAW, :]
            hi, lo = w_hi[:, v % SPL, :], w_lo[:, v % SPL, :]
            if kind == ROWS:
                return slot[:, (v % 2) * HALF:(v % 2 + 1) * HALF], hi, lo
            if kind == COLS:
                src = slot.rearrange("p (k f) -> p k f", k=KD)[:, :, (v % 2) * P:(v % 2 + 1) * P]
                return src, *(m.rearrange("p (k f) -> p k f", k=KD) for m in (hi, lo))
            if kind == PAIRED:
                src = slot.rearrange("p (h k i d) -> p i k h d", k=KD, h=2, i=2)[:, v % 2]
                return src, *(m.rearrange("p (k h d) -> p k h d", k=KD, h=2) for m in (hi, lo))
            return slot[:, (v % 2) * 512:(v % 2 + 1) * 512], hi[:, 0:512], lo[:, 0:512]

        FFN_HALVES = 2 * 3 * NJ
        LOOP_HALVES = 2 * 6
        LOOPS = (NJ - 3) // 2

        @block.sync
        def _(sp):
            def load(u, src, i=None):
                slot = u % RAW
                if u >= RAW:
                    ready = 2 * (u - RAW) + 2
                    sp.wait_ge(sem["lo_ready"], ready if i is None else ready + LOOP_HALVES * i)
                kind = units[u][0]
                if kind == RANK:
                    dst = raw[:, slot, 0:HALF].rearrange("p (k f) -> p k f", k=KD)
                elif kind == PAIRED:
                    for h in range(2):
                        dst = raw[:, slot, h * HALF:(h + 1) * HALF].rearrange("p (k c) -> p k c", k=KD)
                        sp.dma_start(dst, src[:, :, h, :]).then_inc(raw_ready[slot], 16)
                    return
                elif kind == ROWS:
                    dst = raw[:, slot, :].rearrange("p (s n) -> p s n", s=2)
                else:
                    dst = raw[:, slot, :].rearrange("p (k f) -> p k f", k=KD)
                sp.dma_start(dst, src).then_inc(raw_ready[slot], 16)

            u = 0
            done = 0
            while u < len(units):
                if done < len(ffns) and u == ffns[done][0]:
                    _, gate, up, down = ffns[done]
                    done += 1
                    gate_v, up_v = (m.rearrange("(k p) f -> p k f", p=P) for m in (gate, up))
                    for n in range(5):
                        load(u + n, units[u + n][1])
                        if u + n == 0:
                            sp.dma_start(x[:, :, :], a["x"][0].rearrange("(t p) d -> p t d", p=P))\
                                .then_inc(sem["x_loaded"], 16)
                    with sp.Fori(0, LOOPS) as i:
                        for s in range(2):
                            c0 = i * (2 * UC) + (2 + s) * UC
                            load(u + 5 + 3 * s, gate_v[:, :, bass.ds(c0, UC)], i)
                            load(u + 6 + 3 * s, up_v[:, :, bass.ds(c0, UC)], i)
                            r0 = i * (2 * UC) + (1 + s) * UC
                            load(u + 7 + 3 * s, down[bass.ds(r0, UC), :].rearrange("(s p) n -> p s n", p=P), i)
                    for n in range(5 + 6 * LOOPS, 3 * NJ):
                        load(u + n, units[u + n][1])
                    u += 3 * NJ
                else:
                    load(u, units[u][1])
                    u += 1
            for t in range(NT):
                sp.wait_ge(sem["result_ready"], t + 1)
                sp.dma_start(out[0].rearrange("(t p) d -> p t d", p=P)[:, t, :], result[:, t, :]).then_inc(sem["out_stored"], 16)
            sp.wait_ge(sem["out_stored"], 16 * NT)

        @block.gpsimd
        def _(pool):
            pool.memset(ident[:, :], 0.0).then_inc(sem["pool_const"], 1)
            pool.memset(flip, 0.0).then_inc(sem["pool_const"], 1)
            pool.memset(spread[:, :], MASKED).then_inc(sem["pool_const"], 1)
            pool.memset(unit_sq[:, :], 1.0).then_inc(sem["pool_const"], 1)
            pool.wait_ge(sem["pool_const"], 4)
            pool.affine_select(out=ident[:, :], in_=ident[:, :], compare_op=ALU.not_equal, fill=1.0, base=0,
                               pattern=[[-1, P]], channel_multiplier=1).then_inc(sem["pool_const"], 1)
            pool.affine_select(out=flip, in_=flip, compare_op=ALU.not_equal, fill=1.0, base=1 - P,
                               pattern=[[1, P]], channel_multiplier=1).then_inc(sem["pool_const"], 1)
            pool.memset(rank_w[:, :], 0.0).then_inc(sem["rank_zero"], 1)
            pool.wait_ge(sem["table_loaded"], 16)
            starts = bucket_starts()
            for b in range(32):
                lo, hi = 256 - starts[b + 1], 256 - starts[b]
                last = pool.tensor_copy(spread[:, lo:hi], table[:, b:b + 1].to_broadcast([8, hi - lo]))
                last.then_inc(sem["spread_ready"], 1)
            pool.wait_ge(sem["spread_ready"], 32)
            pool.dma_start(spread_dram, spread[:, :]).then_inc(sem["spread_stored"], 16)
            for name, n, at in VECTORS[1:]:
                pool.dma_start(col_rows[at % P:at % P + n, at // P, :], rows_of_vector(a[name]))\
                    .then_inc(sem["vectors_loaded"], 16)
            pool.wait_ge(sem["spread_stored"], 16)
            pool.dma_start(bias_rev, bass.AP(spread_dram.tensor, 0, [[1, P], [384, 8], [1, T]]))\
                .then_inc(sem["bias_rev_loaded"], 16)
            pool.wait_ge(sem["bias_ready"], 4)
            pool.dma_start(bias_dram, bias[:, :, :].rearrange("p h c -> p (h c)")).then_inc(sem["bias_stored"], 16)
            pool.wait_ge(sem["bias_stored"], 16)
            pool.affine_select(out=bias[:, :, :], in_=bias[:, :, :], compare_op=ALU.is_gt, fill=MASKED, base=0,
                               pattern=[[0, 8], [1, T]], channel_multiplier=-1).then_inc(sem["bias_masked"], 1)
            pool.wait_ge(sem["scale_ready"], 2)
            for n, m in enumerate((conv_c[:, 0, :], conv_u, conv_c[:, 1, :], conv_u, conv_b[:, 0, :], conv_b[:, 1, :])):
                pool.wait_ge(sem["nat_sb"], 2 + n)
                m = m.rearrange("p (s t) -> p s t", s=2)
                pool.tensor_tensor(m, m, scale_row[:, None, :].to_broadcast([P, 2, T]), ALU.mult)\
                    .then_inc(sem["scaled"], 1)
            pool.wait_ge(sem["max_ready"], 6)
            pool.dma_start(bias[:, :, :].rearrange("p h c -> p (h c)"), bias_dram).then_inc(sem["bias_loaded"], 16)
            pool.wait_ge(sem["half_done"], 2 * ffns[3][0])
            made = 0

            def constant(ins):
                nonlocal made
                made += 1
                ins.then_inc(sem["gla_const"], 1)
                pool.wait_ge(sem["gla_const"], made)

            for m, value in ((ones, 1.0 / 512), (low_mask, 1.0), (up_mask, 1.0), (reset, 1.0),
                             (score[:, :, :], 0.0)):
                constant(pool.memset(m, value))
            for m, mult, stp, base in ((low_mask, -1, 1, 1), (up_mask, 1, -1, 0)):
                constant(pool.affine_select(out=m, in_=m, compare_op=ALU.is_gt, fill=0.0, base=base,
                                            pattern=[[stp, P]], channel_multiplier=mult))
            constant(pool.memset(low_mask[0:64, 64:128], 0.0))
            constant(pool.memset(up_mask[64:128, 0:64], 0.0))
            constant(pool.memset(reset.rearrange("p (c n) -> p c n", n=64)[:, :, 0:1], 0.0))
            for tile in range(DVE_TILES, 4):
                hi, lo = (memT_hi, memT_lo) if tile == 2 else (yT_hi, yT_lo)
                for m, first, n in ((hi, 0, 16), (lo, 16, CONV_TAPS - 16)):
                    m = m[:, :, :].rearrange("p k t -> p (k t)").bitcast(F32)
                    with pool.Fori(0, n) as j:
                        tap = cols[:, bass.ds(4 * j + (COL_OF["conv_w_2"] + 4 * first + tile), 1)]
                        pool.tensor_tensor(m[:, bass.ds(j * P, P)], ident[:, :], tap.to_broadcast([P, P]), ALU.mult)\
                            .then_inc(sem["tap_diags"], 1)
            pool.wait_ge(sem["scale_ready"], 10)
            for n in range(2):
                pool.wait_ge(sem["nat_sb"], NAT_BEFORE_2 + 1 + 2 * n)
                m = glu[:, 2 * n:2 * n + 2, PAD:PAD + T]
                pool.tensor_tensor(m, m, scale_row[:, None, :].to_broadcast([P, 2, T]), ALU.mult)\
                    .then_inc(sem["scaled"], 1)

        N_GLA_CONST = 5 + 2 + 3

        @block.scalar
        def _(act):
            c = Counter(act, sem)
            v_next = [0]

            def split(i=None, v=None):
                v = v_next[0] if v is None else v
                if v >= n_half:
                    return
                slot = (v // 2) % RAW
                if v % 2 == 0:
                    need = landed[v // 2]
                    act.wait_ge(raw_ready[slot], need if i is None else need + 16 * LOOP_HALVES // 2 // RAW * i)
                if v >= SPL:
                    need = v - SPL + 1
                    act.wait_ge(sem["half_done"], need if i is None else need + LOOP_HALVES * i)
                src, hi, _ = raw_half(v)
                act.activation(hi, src, ACT.Copy).then_inc(sem["hi_ready"], 1)
                if i is None:
                    v_next[0] += 1

            def splits(n):
                for _ in range(n):
                    split()

            def mean_square(t, src=x, dst=mean_sq):
                if c.seen["mean_sq"]:
                    act.wait_ge(sem["mean_sq"], c.seen["mean_sq"])
                c.skip("mean_sq", 1)
                act.activation(junk, src[:, t, :], ACT.Square, scale=1.0 / 32,
                               accum_out=dst[:, t:t + 1]).then_inc(sem["mean_sq"], 1)

            def gain_of(gain, k):
                return both_gains[:, k:k + 1] if gain == "both" else cols[:, gain + k:gain + k + 1]

            def xT_his(gain, hi, by_bank=False):
                for k in range(KD):
                    if by_bank:
                        if k % 2 == 0:
                            c.next("xT_psum")
                        src = bank[:, 4 + k // 2, (k % 2) * T:(k % 2 + 1) * T]
                    else:
                        c.next("xT_psum")
                        src = bank[:, k, 0:T]
                    last = act.activation(hi[:, k, :], src, ACT.Copy, scale=gain_of(gain, k))
                    if not by_bank or k % 2:
                        last.then_inc(sem["xT_hi_ready"], 1)

            def norm(gain, loaded=False):
                if not loaded:
                    c.next("residual", 2)
                    mean_square(0)
                xT_his(gain, xT_hi)
                if not loaded:
                    c.next("residual", 2)
                else:
                    mean_square(0)
                mean_square(1)

            def ffn_step(f, j, i=None):
                g_half = f.v0 + (4 + 6 * (j - 1) if j else 0)
                plus = (lambda k, n: k if i is None else k + n * i)
                jb = j % 2
                n_splits = 6 if 0 < j < NJ - 1 else (4 if j == 0 else 8)
                base = g_half + LEAD
                for n in range(2):
                    split(i, base + n)
                act.wait_ge(sem["gate_scaled"], plus(f.j0 + j + 1, 2))
                act.activation(act_gate[:, jb, :], act_gate[:, jb, :], ACT.Silu).then_inc(sem["act_gate_ready"], 1)
                for n in range(2, 4 if j else 2):
                    split(i, base + n)
                act.wait_ge(sem["hidden_ready"], plus(f.j0 + j + 1, 2))
                act.activation(hid_hi[:, 2 * jb:2 * jb + 2, :], hidden[:, jb, :].rearrange("p (s t) -> p s t", s=2),
                               ACT.Copy).then_inc(sem["hidden_hi_ready"], 1)
                for n in range(4 if j else 2, n_splits):
                    split(i, base + n)
                if i is None:
                    v_next[0] = base + n_splits

            def memory_norm():
                act.wait_ge(sem["mem_loaded"], 16)
                for t in range(NT):
                    mean_square(t, mem_in, mem_sq)
                xT_his(COL_OF["mem"], memT_hi, by_bank=True)

            class Ffn:
                pass

            n_ffn = [0]

            def ffn():
                f = Ffn()
                f.v0, f.j0 = 2 * ffns[n_ffn[0]][0], NJ * n_ffn[0]
                assert v_next[0] == f.v0 + LEAD
                n_ffn[0] += 1
                ffn_step(f, 0)
                if n_ffn[0] == 1:
                    memory_norm()
                if n_ffn[0] == 6:
                    y_hi(1, lambda n: (yT_hi[:, 0:2, :], halves(bank[:, 5, :])))
                ffn_step(f, 1)
                with act.Fori(0, LOOPS) as i:
                    ffn_step(f, 2, i)
                    ffn_step(f, 3, i)
                ffn_step(f, NJ - 1)
                assert v_next[0] == f.v0 + FFN_HALVES + LEAD

            def evac(n, dst, b, func=ACT.Copy, src=None):
                act.wait_ge(sem["half_done"], n)
                src = bank[:, b, :] if src is None else src
                act.activation(dst, src, func).then_inc(sem["nat_sb"], 1)

            def evac_nat(n, dst, b, func=ACT.Copy):
                act.wait_ge(sem["half_done"], n)
                for t in range(NT):
                    last = act.activation(dst[:, t, :], halves(bank[:, b, :])[:, t, :], func, scale=rstd[:, t:t + 1])
                last.then_inc(sem["nat_sb"], 1)

            def halves(m):
                return m.rearrange("p (s t) -> p s t", s=2)

            def softmax_exp(groups, sinks, scale=1.0, from_psum=False):
                for g, (t, heads, nk) in enumerate(groups):
                    c.next("max_ready")
                    for n in range(len(heads)):
                        m = 4 * g + n
                        dst = prob[:, g, n * nk:(n + 1) * nk]
                        src = bank[:, g, n * nk:(n + 1) * nk] if from_psum else dst
                        last = act.activation(dst, src, ACT.Exp, bias=neg_max[:, m:m + 1], scale=scale,
                                              accum_out=den[:, m:m + 1])
                    if sinks:
                        nh = len(heads)
                        last = act.activation(sink_e[:, 4 * g:4 * g + nh], sink_in[:, 4 * g:4 * g + nh], ACT.Exp)
                    last.then_inc(sem["exp_ready"], 1)
                    yield g

            def probT_copies(groups, which):
                for g in range(len(groups)):
                    c.next("probT_psum")
                    if g % 2 == which:
                        act.activation(probT[:, g, :], bank[:, (len(groups) + g) % 8, :], ACT.Copy)\
                            .then_inc(sem["probT_even"], 1)

            def y_hi(n_banks, dst):
                for n in range(n_banks):
                    c.next("out_psum")
                    d, s = dst(n)
                    act.activation(d, s, ACT.Copy).then_inc(sem["y_hi_ready"], 1)

            name, n, at = VECTORS[0]
            act.dma_start(col_rows[at:at + n, 0, :], rows_of_vector(a[name])).then_inc(sem["first_gains_loaded"], 16)
            with nc.allow_non_contiguous_dma(reason="32 x 8 table"):
                act.dma_start(table[:, :], a["rel_bias"].rearrange("b h -> h b")).then_inc(sem["table_loaded"], 16)
            act.dma_start(mem_in[:, :, :], a["mem"][0].rearrange("(t p) d -> p t d", p=P)).then_inc(sem["mem_loaded"], 16)
            act.dma_start(sink, a["ev_sinks"].to_broadcast([P, 8])).then_inc(sem["sinks_loaded"], 16)
            act.dma_start(gain_row[:, :], a["final_norm"].rearrange("(a n) -> a n", a=1).to_broadcast([P, D]))\
                .then_inc(sem["gain_loaded"], 16)
            act.wait_ge(sem["rank_zero"], 1)
            act.dma_start(rank_w[P - GATE_RANK:P, :], a["gate_w_up_2"][0]).then_inc(sem["rank_loaded"], 16)

            splits(2)
            act.wait_ge(sem["x_loaded"], 16)
            norm(COL_OF["ffn1"], loaded=True)
            splits(LEAD - 2)
            ffn()
            norm(COL_OF["mix"])
            v = v_next[0] - LEAD
            splits(4)
            act.wait_ge(sem["half_done"], v + 6)
            for t in range(NT):
                last = act.activation(swa_v[:, t, :], bank[:, 3, t * P:(t + 1) * P], ACT.Copy,
                                      scale=rstd[:, t:t + 1])
            last.then_inc(sem["nat_sb"], 1)
            splits(2)
            soft = softmax_exp(SWA_GROUPS, True)
            evac(v + 8, conv_c[:, 0, :], 6)
            splits(2)
            evac(v + 10, conv_u, 7)
            splits(2)
            next(soft)
            next(soft)
            evac(v + 12, conv_c[:, 1, :], 6)
            splits(2)
            next(soft)
            act.wait_ge(sem["conv_v_ready"], 1)
            evac(v + 14, conv_u, 7)
            splits(2)
            next(soft)
            evac(v + 16, conv_b[:, 0, :], 6)
            splits(2)
            next(soft)
            next(soft)
            evac(v + 18, conv_b[:, 1, :], 7)
            probT_copies(SWA_GROUPS, 0)
            y_hi(2, lambda n: (yT_hi[:, 4:8, n * P:(n + 1) * P], bank[:, 4 + n, :].rearrange("p (i q) -> p i q", i=4)))
            splits(2)
            for n in range(2):
                act.wait_ge(sem["conv_ready"], n + 1)
                act.activation(yT_hi[:, 2 * n:2 * n + 2, :], halves(conv_y[:, n, :]), ACT.Copy).then_inc(sem["y_hi_ready"], 1)
            splits(8)

            def cross(l, kv):
                norm(COL_OF["xa"] + KD * l)
                v = v_next[0] - LEAD
                splits(4)
                soft = softmax_exp(XA_GROUPS, False, 128.0 ** -0.5, from_psum=True)
                if kv:
                    mem_kv(4, lambda n: [next(soft) for _ in range(4 if n == 1 else 0)], (0, 1, 2))
                else:
                    for _ in soft:
                        pass
                probT_copies(XA_GROUPS, 0)
                y_hi(2, lambda n: (yT_hi[:, 0:4, n * P:(n + 1) * P], bank[:, n, :].rearrange("p (i q) -> p i q", i=4)))
                splits(6 if kv else 4)

            def mem_kv(b0, between, split_after):
                v = v_next[0] - LEAD
                for n in range(4):
                    b = b0 + n % 2 if b0 == 6 else b0 + n
                    if n < 2:
                        evac(v + 2 + 2 * n, mem_k[:, 2 * n:2 * n + 2, :], b, src=halves(bank[:, b, :]))
                    else:
                        evac(v + 2 + 2 * n, mem_v[:, :, (n - 2) * T:(n - 1) * T], b, src=halves(bank[:, b, :]))
                    if n in split_after:
                        splits(2)
                    between(n)

            cross(0, True)
            norm(COL_OF["ffn2"])
            ffn()
            norm(COL_OF["ffn1"] + KD)
            ffn()
            norm(COL_OF["mix"] + KD)
            v = v_next[0] - LEAD
            splits(12)
            for n in range(2):
                evac_nat(v + 14 + 2 * n, v_sb[:, :, n * T:(n + 1) * T], 6 + n)
                splits(2)
            soft = softmax_exp(MOBA_GROUPS, False)
            mem_kv(6, lambda n: next(soft), (0, 1, 2))
            for _ in soft:
                pass
            probT_copies(MOBA_GROUPS, 0)
            y_hi(4, lambda n: (yT_hi[:, 4 * (n % 2):4 * (n % 2) + 4, (n // 2) * P:(n // 2 + 1) * P],
                               bank[:, 4 + n, :].rearrange("p (i q) -> p i q", i=4)))
            splits(10)
            cross(1, False)
            norm(COL_OF["ffn2"] + KD)
            ffn()
            norm("both")
            for t in range(NT):
                c.next("residual", 2)
                mean_square(t)
            act.dma_start(gain_row[:, :], a["final_norm_2"].rearrange("(a n) -> a n", a=1).to_broadcast([P, D]))\
                .then_inc(sem["gain_loaded"], 16)
            act.dma_start(gla_gain, a["gla_norm_2"].to_broadcast([P, 512])).then_inc(sem["gla_gain_loaded"], 16)
            ffn()
            norm(COL_OF["mix_2"])
            v = v_next[0] - LEAD
            splits(4)
            c.next("decays")
            act.activation(g_l, g_l, ACT.Exp).then_inc(sem["act_step"], 1)
            c.next("act_step")
            act.activation(g_l, g_l, ACT.Ln, bias=1.0).then_inc(sem["act_step"], 1)
            c.next("act_step")
            splits(2)
            c.next("decays")
            act.activation(e_pos, g_cum, ACT.Exp, scale=1.0 / 16)
            act.activation(e_neg, g_cum, ACT.Exp, scale=-1.0 / 16).then_inc(sem["act_step"], 1)
            c.next("act_step")
            c.next("decays")
            act.activation(e_end, e_end, ACT.Exp, scale=1.0 / 16)
            act.activation(decay, decay_in, ACT.Exp, scale=1.0 / 16).then_inc(sem["act_step"], 1)
            c.next("act_step")
            for n in range(2):
                evac(v + 8 + 4 * n, glu[:, 2 * n:2 * n + 2, PAD:PAD + T], 1 + 2 * n, src=halves(bank[:, 1 + 2 * n, :]))
                splits(2)
                act.wait_ge(sem["proj_sb"], PROJ_BEFORE_2 + 4 + n)
                m = sig_b[:, 2 * n:2 * n + 2, :]
                act.activation(m, m, ACT.Sigmoid).then_inc(sem["nat_sb"], 1)
                splits(2)
            for n in range(2):
                evac_nat(v + 16 + 2 * n, g_v[:, :, n * T:(n + 1) * T], (7, 0)[n])
                splits(2)
            for n in range(2):
                evac_nat(v + 20 + 2 * n, g_r[:, :, n * T:(n + 1) * T], 1 + n, func=ACT.Silu)
                splits(2)
            c.next("k_nat_psum")
            act.activation(k_nat, bank[:, 4, :], ACT.Copy).then_inc(sem["k_nat_ready"], 1)

            def conv_evac(tile, b):
                c.next("conv_psum")
                at = COL_OF["conv_b_2"] + tile
                act.activation(conv_acc[:, tile, :], bank[:, b, 0:T], ACT.Identity, bias=cols[:, at:at + 1])\
                    .then_inc(sem["conv_evac"], 1)

            conv_evac(2, 5)
            c.next("out_psum")
            for h in range(2):
                act.activation(score[:, h, :], bank[:, h, :], ACT.Square).then_inc(sem["o_square"], 1)
            conv_evac(3, 6)
            y_hi(2, lambda n: (yT_hi[:, 4 + 2 * n:6 + 2 * n, :], halves(bank[:, 2 + n, :])))
            c.next("var_in")
            act.activation(sq_c[:, :, :], centred[:, :, :], ACT.Square).then_inc(sem["var_in"], 1)
            splits(3)
            for pair in (slice(0, 2), slice(2, 4)):
                c.next("ln_ready")
                for n in range(pair.start, pair.stop):
                    g, b = COL_OF["ln_g_2"] + n, COL_OF["ln_b_2"] + n
                    last = act.activation(conv_acc[:, n, :], centred[:, n, :], ACT.Silu, scale=cols[:, g:g + 1],
                                          bias=cols[:, b:b + 1])
                last.then_inc(sem["act_step"], 1)
                c.next("act_step")
                act.activation(yT_hi[:, pair, :], conv_acc[:, pair, :], ACT.Copy).then_inc(sem["y_hi_ready"], 1)
            splits(5)
            act.dma_start(p_in[:, :, :], a["p_2"][0, 0].rearrange("(t p) c -> p t c", p=P)).then_inc(sem["p_loaded"], 16)
            norm(COL_OF["ffn2_2"])
            ffn()
            norm(COL_OF["ple_2"])
            v = v_next[0] - LEAD
            act.wait_ge(sem["half_done"], v + 2)
            for t in range(NT):
                act.activation(p_out[:, t, :], bank[:, 2 * t:2 * t + 2, :].rearrange("p a c -> p (a c)"), ACT.Copy)\
                    .then_inc(sem["nat_sb"], 1)
            splits(10)
            for t in range(NT):
                for n in range(2):
                    if t == 1 and n == 1:
                        act.wait_ge(sem["half_done"], n_half)
                    else:
                        act.wait_ge(sem["acc_ready"], ACC_BEFORE_PLE + 2 * t + n + 1)
                    act.activation(ple_gate[:, t, n * 512:(n + 1) * 512], d_bank(t, n), ACT.Sigmoid,
                                   scale=rstd[:, t:t + 1]).then_inc(sem["nat_sb"], 1)
            for t in range(NT):
                c.next("residual", 2)
                mean_square(t)

        @block.vector
        def _(dve):
            c = Counter(dve, sem)
            v_next = [0]

            def link(ins, name="dve_step"):
                ins.then_inc(sem[name], 1)
                c.next(name)

            def split(i=None, v=None):
                v = v_next[0] if v is None else v
                if v >= n_half:
                    return
                dve.wait_ge(sem["hi_ready"], v + 1 if i is None else v + 1 + LOOP_HALVES * i)
                src, hi, lo = raw_half(v)
                dve.tensor_tensor(lo, src, hi.bitcast(F32), ALU.subtract).then_inc(sem["lo_ready"], 1)
                if i is None:
                    v_next[0] += 1

            def splits(n):
                for _ in range(n):
                    split()

            def rsqrt(dst, src, tmp, tmp2):
                link(dve.tensor_scalar(src, src, EPS, None, ALU.add))
                link(dve.tensor_scalar(tmp.bitcast(U32), src.bitcast(U32), 1, None, ALU.logical_shift_right))
                link(dve.tensor_scalar(dst.bitcast(U32), tmp.bitcast(U32), -1.0, float(0x5F3759DF), ALU.mult, ALU.add))
                link(dve.tensor_tensor(tmp, dst, dst, ALU.mult))
                link(dve.tensor_tensor(tmp, tmp, src, ALU.mult))
                link(dve.scalar_tensor_tensor(tmp2, tmp, -10.0 / 3, tmp, ALU.add, ALU.mult))
                link(dve.tensor_scalar(tmp2, tmp2, 0.375, 1.875, ALU.mult, ALU.add))
                link(dve.tensor_tensor(dst, tmp2, dst, ALU.mult))
                link(dve.tensor_tensor(tmp, dst, dst, ALU.mult))
                link(dve.scalar_tensor_tensor(tmp, tmp, -0.5, src, ALU.mult, ALU.mult))
                link(dve.scalar_tensor_tensor(dst, tmp, 1.5, dst, ALU.add, ALU.mult))

            def rstd_of_both():
                c.next("mean_sq", 2)
                rsqrt(rstd, mean_sq, small[:, 4:6], small[:, 6:8])

            def gain_of(gain, k):
                return both_gains[:, k:k + 1] if gain == "both" else cols[:, gain + k:gain + k + 1]

            def xT_los(gain, hi, lo, by_bank=False):
                for k in range(KD):
                    if by_bank:
                        if k % 2 == 0:
                            c.next("xT_hi_ready")
                        src = bank[:, 4 + k // 2, (k % 2) * T:(k % 2 + 1) * T]
                    else:
                        c.next("xT_hi_ready")
                        src = bank[:, k, 0:T]
                    last = dve.scalar_tensor_tensor(lo[:, k, :], src, gain_of(gain, k),
                                                    hi[:, k, :].bitcast(F32), ALU.mult, ALU.subtract)
                    if not by_bank or k % 2:
                        last.then_inc(sem["xT_lo_ready"], 1)

            def norm(gain):
                xT_los(gain, xT_hi, xT_lo)
                rstd_of_both()
                if gain == "both":
                    final_norm()
                for t in range(NT):
                    last = dve.tensor_scalar(diag[:, t, :], ident[:, :], rstd[:, t:t + 1], None, ALU.mult)
                last.then_inc(sem["diag_ready"], 1)

            def final_norm():
                dve.wait_ge(sem["gain_loaded"], 16)
                for t in range(NT):
                    for n in range(2):
                        part = slice(n * 512, (n + 1) * 512)
                        dve.scalar_tensor_tensor(x[:, t, part], x[:, t, part], rstd[:, t:t + 1], gain_row[:, part],
                                                 ALU.mult, ALU.mult).then_inc(sem["residual"], 1)
                link(dve.tensor_copy(first_rstd, rstd))
                rstd_of_both()
                link(dve.tensor_tensor(rstd, rstd, first_rstd, ALU.mult))

            def scale_copy(b):
                c.next("scale_psum")
                link(dve.tensor_copy(scale_row[:, :], bank[:, b, 0:T]), "scale_ready")

            def scaled(n, dst, b):
                dve.wait_ge(sem["half_done"], n)
                dve.tensor_tensor(dst, halves(bank[:, b, :]), scale_row[:, None, :].to_broadcast([P, 2, T]), ALU.mult)\
                    .then_inc(sem["proj_sb"], 1)

            def add_residual(scale, n_done):
                for t in range(NT):
                    for n in range(2):
                        if t == 1 and n == 1:
                            dve.wait_ge(sem["half_done"], n_done)
                        else:
                            c.next("acc_ready")
                        part = x[:, t, n * 512:(n + 1) * 512]
                        dve.scalar_tensor_tensor(part, d_bank(t, n), scale, part, ALU.mult, ALU.add)\
                            .then_inc(sem["residual"], 1)

            def ffn_step(f, j, i=None):
                g_half = f.v0 + (4 + 6 * (j - 1) if j else 0)
                plus = (lambda k, n: k if i is None else k + n * i)
                jb = j % 2
                n_splits = 6 if 0 < j < NJ - 1 else (4 if j == 0 else 8)
                base = g_half + LEAD
                if j == 0:
                    split(i, base)
                    scale_copy(4)
                both = scale_row[:, None, :].to_broadcast([P, 2, T])
                dve.wait_ge(sem["half_done"], plus(g_half + 2, LOOP_HALVES))
                dve.tensor_tensor(halves(act_gate[:, jb, :]), halves(bank[:, 2 * jb, :]), both, ALU.mult)\
                    .then_inc(sem["gate_scaled"], 1)
                for n in range(1 if j == 0 else 0, 2):
                    split(i, base + n)
                dve.wait_ge(sem["half_done"], plus(g_half + 4, LOOP_HALVES))
                dve.tensor_tensor(halves(hidden[:, jb, :]), halves(bank[:, 2 * jb + 1, :]), both, ALU.mult)\
                    .then_inc(sem["up_scaled"], 1)
                dve.wait_ge(sem["up_scaled"], plus(f.j0 + j + 1, 2))
                dve.wait_ge(sem["act_gate_ready"], plus(f.j0 + j + 1, 2))
                dve.tensor_tensor(hidden[:, jb, :], act_gate[:, jb, :], hidden[:, jb, :], ALU.mult)\
                    .then_inc(sem["hidden_ready"], 1)
                for n in range(2, 4 if j else 2):
                    split(i, base + n)
                dve.wait_ge(sem["hidden_hi_ready"], plus(f.j0 + j + 1, 2))
                dve.tensor_tensor(hid_lo[:, 2 * jb:2 * jb + 2, :], hidden[:, jb, :].rearrange("p (s t) -> p s t", s=2),
                                  hid_hi[:, 2 * jb:2 * jb + 2, :].bitcast(F32), ALU.subtract)\
                    .then_inc(sem["hidden_lo_ready"], 1)
                for n in range(4 if j else 2, n_splits):
                    split(i, base + n)
                if i is None:
                    v_next[0] = base + n_splits

            class Ffn:
                pass

            n_ffn = [0]

            def ffn():
                f = Ffn()
                f.v0, f.j0 = 2 * ffns[n_ffn[0]][0], NJ * n_ffn[0]
                n_ffn[0] += 1
                ffn_step(f, 0)
                if n_ffn[0] == 1:
                    memory_norm()
                    for n in range(4):
                        c.next("bias_psum")
                        dve.tensor_copy(bias[:, 2 * n:2 * n + 2, :], halves(bank[:, 4 + n, :]))\
                            .then_inc(sem["bias_ready"], 1)
                if n_ffn[0] == 6:
                    y_lo(1, lambda n: (yT_lo[:, 0:2, :], halves(bank[:, 5, :]), yT_hi[:, 0:2, :]))
                ffn_step(f, 1)
                with dve.Fori(0, LOOPS) as i:
                    ffn_step(f, 2, i)
                    ffn_step(f, 3, i)
                ffn_step(f, NJ - 1)
                add_residual(0.5, f.v0 + FFN_HALVES)

            def halves(m):
                return m.rearrange("p (s t) -> p s t", s=2)

            def logits(groups, sinks, scale, biased):
                for g, (t, heads, nk) in enumerate(groups):
                    c.next("scores")
                    nh = len(heads)
                    m = slice(4 * g, 4 * g + nh)
                    if biased:
                        dst = prob[:, g, :].rearrange("p (h k) -> p h k", k=nk)
                        link(dve.scalar_tensor_tensor(dst, bank[:, g, :].rearrange("p (h k) -> p h k", k=nk), scale,
                                                      bias[:, heads[0]:heads[0] + nh, T - nk:T], ALU.mult, ALU.add))
                        link(dve.tensor_reduce(top[:, m], dst, AX.X, ALU.max))
                    else:
                        link(dve.tensor_reduce(top[:, m], bank[:, g, :].rearrange("p (h k) -> p h k", k=nk), AX.X,
                                               ALU.max))
                    if sinks:
                        link(dve.scalar_tensor_tensor(neg_max[:, m], top[:, m], -1.0,
                                                      neg_sink[:, heads[0]:heads[0] + nh], ALU.mult, ALU.min))
                        dve.tensor_tensor(sink_in[:, m], sink[:, heads[0]:heads[0] + nh], neg_max[:, m], ALU.add)\
                            .then_inc(sem["max_ready"], 1)
                    else:
                        dve.tensor_scalar(neg_max[:, m], top[:, m], -1.0 if biased else -scale, None, ALU.mult)\
                            .then_inc(sem["max_ready"], 1)
                    yield g

            def normalise(groups, sinks):
                for g, (t, heads, nk) in enumerate(groups):
                    c.next("exp_ready")
                    nh = len(heads)
                    m = slice(4 * g, 4 * g + nh)
                    if sinks:
                        link(dve.tensor_tensor(den[:, m], den[:, m], sink_e[:, m], ALU.add))
                    link(dve.reciprocal(inv[:, m], den[:, m]))
                    for n in range(nh):
                        p = prob[:, g, n * nk:(n + 1) * nk]
                        last = dve.tensor_scalar(p, p, inv[:, 4 * g + n:4 * g + n + 1], None, ALU.mult)
                    last.then_inc(sem["probs_ready"], 1)
                    yield g

            def probT_copies(groups, which):
                for g in range(len(groups)):
                    c.next("probT_psum")
                    if g % 2 == which:
                        dve.tensor_copy(probT[:, g, :], bank[:, (len(groups) + g) % 8, :]).then_inc(sem["probT_odd"], 1)

            def y_lo(n_banks, dst):
                for n in range(n_banks):
                    c.next("y_hi_ready")
                    lo, src, hi = dst(n)
                    dve.tensor_tensor(lo, src, hi.bitcast(F32), ALU.subtract).then_inc(sem["y_lo_ready"], 1)

            def memory_norm():
                c.next("mean_sq", 2)
                rsqrt(mem_rstd, mem_sq, small[:, 4:6], small[:, 6:8])
                for t in range(NT):
                    dve.tensor_scalar(mem_in[:, t, :], mem_in[:, t, :], mem_rstd[:, t:t + 1], None, ALU.mult)\
                        .then_inc(sem["mem_normed"], 1)
                c.next("vectors_psum")
                link(dve.tensor_copy(cols[:, 0:N_COLS], bank[:, 7, 0:N_COLS]))
                g = COL_OF["ffn1_2"]
                link(dve.tensor_tensor(both_gains, cols[:, g:g + KD], bank[:, 7, T:T + KD], ALU.mult), "cols_ready")
                xT_los(COL_OF["mem"], memT_hi, memT_lo, by_bank=True)

            dve.wait_ge(sem["first_gains_psum"], 1)
            link(dve.tensor_copy(cols[:, 0:16], bank[:, 7, 256:272]), "cols_ready")
            splits(2)
            norm(COL_OF["ffn1"])
            splits(LEAD - 2)
            ffn()
            norm(COL_OF["mix"])
            v = v_next[0] - LEAD
            for n in range(2):
                link(dve.memset(conv_v[:, n, 0:2], 0.0))
            dve.wait_ge(sem["sinks_loaded"], 16)
            link(dve.tensor_scalar(neg_sink, sink, -1.0, None, ALU.mult))
            scale_copy(5)
            for n in range(2):
                scaled(v + 2 + 2 * n, q_sb[:, 2 * n:2 * n + 2, :], n)
                splits(2)
            dve.wait_ge(sem["half_done"], v + 6)
            dve.tensor_tensor(swa_k, bank[:, 2, 0:T], scale_row[:, :], ALU.mult).then_inc(sem["proj_sb"], 1)
            splits(2)
            dve.wait_ge(sem["bias_masked"], 1)
            soft = logits(SWA_GROUPS, True, 0.125, True)
            norms = normalise(SWA_GROUPS, True)

            def conv(n):
                dve.wait_ge(sem["scaled"], 2 * n + 2)
                dve.tensor_tensor(conv_v[:, :, 2:2 + T], halves(conv_c[:, n, :]), halves(conv_u), ALU.mult)\
                    .then_inc(sem["conv_v_ready"], 1)
                c.next("conv_v_ready")
                y = halves(conv_y[:, n, :])
                w = COL_OF["conv_w"]
                for i in range(2):
                    ch = 2 * n + i
                    link(dve.tensor_scalar(y[:, i, :], conv_v[:, i, 0:T], cols[:, w + ch:w + ch + 1], None, ALU.mult))
                    for j in (1, 2):
                        wj = w + 4 * j + ch
                        link(dve.scalar_tensor_tensor(y[:, i, :], conv_v[:, i, j:j + T], cols[:, wj:wj + 1],
                                                      y[:, i, :], ALU.mult, ALU.add))

            splits(4)
            next(soft)
            next(soft)
            conv(0)
            next(soft)
            splits(2)
            next(soft)
            next(norms)
            splits(2)
            next(soft)
            next(soft)
            next(norms)
            splits(2)
            for _ in norms:
                pass
            probT_copies(SWA_GROUPS, 1)
            y_lo(2, lambda n: (yT_lo[:, 4:8, n * P:(n + 1) * P], bank[:, 4 + n, :].rearrange("p (i q) -> p i q", i=4),
                               yT_hi[:, 4:8, n * P:(n + 1) * P]))
            conv(1)
            for n in range(2):
                dve.wait_ge(sem["scaled"], 5 + n)
                dve.tensor_tensor(conv_y[:, n, :], conv_y[:, n, :], conv_b[:, n, :], ALU.mult)\
                    .then_inc(sem["conv_ready"], 1)
            split()
            y_lo(2, lambda n: (yT_lo[:, 2 * n:2 * n + 2, :], halves(conv_y[:, n, :]), yT_hi[:, 2 * n:2 * n + 2, :]))
            v = v_next[0] - LEAD
            splits(9)
            add_residual(1.0, v + 9)

            def cross(l, kv):
                norm(COL_OF["xa"] + KD * l)
                v = v_next[0] - LEAD
                scale_copy(7)
                for n in range(2):
                    scaled(v + 2 + 2 * n, q_sb[:, 2 * n:2 * n + 2, :], n)
                    splits(2)
                if kv:
                    splits(4)
                for _ in logits(XA_GROUPS, False, 128.0 ** -0.5, False):
                    pass
                for _ in normalise(XA_GROUPS, False):
                    pass
                if kv:
                    splits(2)
                probT_copies(XA_GROUPS, 1)
                y_lo(2, lambda n: (yT_lo[:, 0:4, n * P:(n + 1) * P], bank[:, n, :].rearrange("p (i q) -> p i q", i=4),
                                   yT_hi[:, 0:4, n * P:(n + 1) * P]))
                v = v_next[0] - LEAD
                rest = 6 if kv else 4
                splits(rest)
                add_residual(1.0, v + rest)

            cross(0, True)
            norm(COL_OF["ffn2"])
            ffn()
            norm(COL_OF["ffn1"] + KD)
            ffn()
            norm(COL_OF["mix"] + KD)
            v = v_next[0] - LEAD
            scale_copy(7)
            for n in range(6):
                scaled(v + 2 + 2 * n, q_sb[:, 2 * n:2 * n + 2, :] if n < 4 else k_sb[:, 2 * n - 8:2 * n - 6, :], n)
                splits(2)
            splits(4)
            dve.wait_ge(sem["bias_loaded"], 16)
            soft = logits(MOBA_GROUPS, False, 128.0 ** -0.5, True)
            norms = normalise(MOBA_GROUPS, False)
            next(soft)
            next(soft)
            splits(2)
            next(soft)
            next(norms)
            splits(2)
            next(soft)
            next(norms)
            splits(2)
            next(soft)
            next(norms)
            next(soft)
            for _ in norms:
                pass
            probT_copies(MOBA_GROUPS, 1)
            y_lo(4, lambda n: (yT_lo[:, 4 * (n % 2):4 * (n % 2) + 4, (n // 2) * P:(n // 2 + 1) * P],
                               bank[:, 4 + n, :].rearrange("p (i q) -> p i q", i=4),
                               yT_hi[:, 4 * (n % 2):4 * (n % 2) + 4, (n // 2) * P:(n // 2 + 1) * P]))
            v = v_next[0] - LEAD
            splits(10)
            add_residual(1.0, v + 10)
            cross(1, False)
            norm(COL_OF["ffn2"] + KD)
            ffn()
            norm("both")
            ffn()
            norm(COL_OF["mix_2"])
            v = v_next[0] - LEAD
            scale_copy(7)
            dve.wait_ge(sem["half_done"], v + 2)
            dve.tensor_tensor(rank_x[:, :], bank[:, 0, 0:T], scale_row[:, :], ALU.mult).then_inc(sem["proj_sb"], 1)
            splits(2)
            scaled(v + 4, halves(g_q), 5)
            link(dve.memset(glu[:, :, 0:PAD], 0.0))
            dve.wait_ge(sem["gla_const"], N_GLA_CONST)
            c.next("rank_psum")
            for i in range(2):
                g = COL_OF["gate_b_2"] + i
                link(dve.tensor_scalar(g_z[:, i * T:(i + 1) * T], bank[:, 7, i * T:(i + 1) * T], cols[:, g:g + 1],
                                       None, ALU.add))
            link(dve.scalar_tensor_tensor(g_l, g_z, -1.0, g_z, ALU.mult, ALU.min), "decays")
            splits(2)
            c.next("act_step", 2)
            link(dve.scalar_tensor_tensor(g_z, g_z, 0.0, g_l, ALU.min, ALU.subtract))
            dve.tensor_tensor_scan(g_cum[:, 0:T], reset, g_z[:, 0:T], 0.0, ALU.mult, ALU.add)
            link(dve.tensor_tensor_scan(g_cum[:, T:2 * T], reset, g_z[:, T:2 * T], 0.0, ALU.mult, ALU.add), "decays")
            chunks = g_cum.rearrange("p (n c) -> p n c", c=64)
            link(dve.tensor_copy(decay_in, chunks[:, :, 63]))
            link(dve.tensor_tensor(e_end.rearrange("p (n c) -> p n c", c=64), decay_in[:, :, None].to_broadcast([P, 8, 64]),
                                   chunks, ALU.subtract), "decays")
            splits(2)
            P1 = PROJ_BEFORE_2
            scaled(v + 6, halves(g_k), 6)
            dve.wait_ge(sem["proj_sb"], P1 + 3)
            c.next("act_step")
            dve.scalar_tensor_tensor(q_dec, g_q, 0.125, e_pos, ALU.mult, ALU.mult)
            dve.tensor_tensor(k_neg, g_k, e_neg, ALU.mult).then_inc(sem["gla_operands"], 1)
            dve.scalar_tensor_tensor(q_neg, g_q, 0.125, e_neg, ALU.mult, ALU.mult)
            dve.tensor_tensor(k_pos, g_k, e_pos, ALU.mult).then_inc(sem["gla_operands"], 1)
            c.next("act_step")
            dve.tensor_tensor(k_end, g_k, e_end, ALU.mult).then_inc(sem["gla_operands"], 1)
            for n in range(2):
                splits(2)
                scaled(v + 10 + 4 * n, sig_b[:, 2 * n:2 * n + 2, :], 2 + 2 * n)
                splits(2)
            for n in range(2):
                dve.wait_ge(sem["nat_sb"], NAT_BEFORE_2 + 2 + 2 * n)
                dve.wait_ge(sem["scaled"], 6 + n + 1)
                s = slice(2 * n, 2 * n + 2)
                link(dve.tensor_tensor(glu[:, s, PAD:PAD + T], glu[:, s, PAD:PAD + T], sig_b[:, s, :], ALU.mult),
                     "glu_ready")
            w = COL_OF["conv_w_2"]
            for n in range(DVE_TILES):
                b = COL_OF["conv_b_2"] + n
                dve.tensor_scalar(conv_acc[:, n, :], glu[:, n, 0:T], cols[:, w + n:w + n + 1], cols[:, b:b + 1],
                                  ALU.mult, ALU.add).then_inc(sem["conv_tap"], 1)

            def taps(lo, hi):
                with dve.Fori(lo, hi) as j:
                    for n in range(DVE_TILES):
                        dve.wait_ge(sem["conv_tap"], DVE_TILES * j + (n + 1 - DVE_TILES))
                        dve.scalar_tensor_tensor(conv_acc[:, n, :], glu[:, n, bass.ds(j, T)],
                                                 cols[:, bass.ds(4 * j + w + n, 1)], conv_acc[:, n, :],
                                                 ALU.mult, ALU.add).then_inc(sem["conv_tap"], 1)

            for n in range(8):
                taps(1 + 3 * n, 4 + 3 * n)
                split()
            c.next("gla_scores", 2)
            for m, b in ((low_mask, 0), (up_mask, 2)):
                for h in range(2):
                    dst = score[:, h, :].rearrange("p (n t) -> p n t", n=4)
                    mask = m.bitcast(U32)[:, None, :].to_broadcast([P, 4, P])
                    link(dve.copy_predicated(dst, mask, bank[:, b + h, :].rearrange("p (n t) -> p n t", n=4)),
                         "score_ready")
            c.next("kv_psum")
            link(dve.tensor_copy(state[:, 0, :], bank[:, 6, 0:T]))
            for i in range(2):
                s = slice(i * P, (i + 1) * P)
                link(dve.scalar_tensor_tensor(state[:, 1, s], state[:, 0, s], decay[:, 4 * i + 1:4 * i + 2],
                                              bank[:, 7, s], ALU.mult, ALU.add))
            for i in range(2):
                s = slice(i * P, (i + 1) * P)
                last = dve.scalar_tensor_tensor(state[:, 2, s], state[:, 1, s], decay[:, 4 * i + 2:4 * i + 3],
                                                bank[:, 6, T + i * P:T + (i + 1) * P], ALU.mult, ALU.add)
            last.then_inc(sem["states_ready"], 1)
            taps(25, CONV_TAPS)
            c.skip("conv_tap", DVE_TILES * CONV_TAPS)
            dve.wait_ge(sem["gla_gain_loaded"], 16)
            dve.wait_ge(sem["nat_sb"], NAT_BEFORE_2 + 8)
            link(dve.tensor_tensor(g_r[:, :, :], g_r[:, :, :], gla_gain[:, None, :].to_broadcast([P, NT, 512]), ALU.mult))
            c.next("o_square", 2)
            for h in range(2):
                link(dve.tensor_reduce(o_ms[:, 4 * h:4 * h + 4], score[:, h, :].rearrange("p (n t) -> p n t", n=4),
                                       AX.X, ALU.add))
            link(dve.tensor_scalar(o_ms, o_ms, 1.0 / P, None, ALU.mult))
            rsqrt(o_rstd, o_ms, small[:, 200:208], small[:, 220:228])
            for h in range(2):
                o = o_nat.rearrange("p t (i h d) -> p h t i d", i=2, h=2)[:, h]
                r = g_r.rearrange("p t (i h d) -> p h t i d", i=2, h=2)[:, h]
                src = bank[:, h, :].rearrange("p (t i d) -> p t i d", t=2, i=2)
                rs = o_rstd[:, 4 * h:4 * h + 4].rearrange("p (t i) -> p t i", t=2)[:, :, :, None]
                link(dve.tensor_tensor(o, src, rs.to_broadcast([P, 2, 2, P]), ALU.mult))
                dve.tensor_tensor(o, o, r, ALU.mult).then_inc(sem["gated"], 1)
            y_lo(2, lambda n: (yT_lo[:, 4 + 2 * n:6 + 2 * n, :], halves(bank[:, 2 + n, :]), yT_hi[:, 4 + 2 * n:6 + 2 * n, :]))
            c.next("mean_psum")
            dve.tensor_tensor(centred[:, :, :], conv_acc[:, :, :], bank[:, 0, None, 0:T].to_broadcast([P, 4, T]),
                              ALU.subtract).then_inc(sem["var_in"], 1)
            v = v_next[0] - LEAD
            splits(2)
            c.next("var_psum")
            link(dve.tensor_copy(k_end[:, 0:T], bank[:, 1, 0:T]))
            rsqrt(ln_rstd, k_end[:, 0:T], k_end[:, T:2 * T], e_end[:, T:2 * T])
            pairs = (slice(0, 2), slice(2, 4))
            for pair in pairs:
                dve.tensor_tensor(centred[:, pair, :], centred[:, pair, :], ln_rstd[:, None, :].to_broadcast([P, 2, T]),
                                  ALU.mult).then_inc(sem["ln_ready"], 1)
            split()
            y_lo(2, lambda n: (yT_lo[:, pairs[n], :], conv_acc[:, pairs[n], :], yT_hi[:, pairs[n], :]))
            splits(5)
            add_residual(1.0, v + 8)
            norm(COL_OF["ffn2_2"])
            ffn()
            norm(COL_OF["ple_2"])
            splits(10)
            for t in range(NT):
                for n in range(2):
                    part = slice(n * 512, (n + 1) * 512)
                    dve.wait_ge(sem["nat_sb"], NAT_BEFORE_2 + 8 + 2 + 2 * t + n + 1)
                    link(dve.tensor_tensor(ple_gate[:, t, part], ple_gate[:, t, part], p_out[:, t, part], ALU.mult))
                    dve.tensor_tensor(x[:, t, part], x[:, t, part], ple_gate[:, t, part], ALU.add)\
                        .then_inc(sem["residual"], 1)
            dve.wait_ge(sem["gain_loaded"], 32)
            rstd_of_both()
            for t in range(NT):
                dve.scalar_tensor_tensor(result[:, t, :], x[:, t, :], rstd[:, t:t + 1], gain_row[:, :],
                                         ALU.mult, ALU.mult).then_inc(sem["result_ready"], 1)

        @block.tensor
        def _(pe):
            c = Counter(pe, sem)
            v_next = [0]

            def split_ready(v, i):
                pe.wait_ge(sem["lo_ready"], v + 1 if i is None else v + 1 + LOOP_HALVES * i)

            def products(dst, lhs, rhs, start, stop):
                for n, (l, r) in enumerate(((0, 0), (0, 1), (1, 0))):
                    last = pe.matmul(dst, lhs[l], rhs[r], start=start and n == 0, stop=stop and n == 2)
                return last

            def w_cols(v, k, n=P):
                return tuple(m[:, v % SPL, k * n:(k + 1) * n] for m in (w_hi, w_lo))

            def xk(xs, k):
                return tuple(m[:, k, :] for m in xs)

            X, Y, MEM, HID = (xT_hi, xT_lo), (yT_hi, yT_lo), (memT_hi, memT_lo), (hid_hi, hid_lo)

            def transposed(v, dst, xs, i=None, first=False):
                split_ready(v, i)
                for k in range(KD):
                    if first:
                        c.next("xT_lo_ready")
                    last = products(dst, w_cols(v, k), xk(xs, k), k == 0, k == KD - 1)
                last.then_inc(sem["half_done"], 1)

            def natural(v, dst, xs, first=False):
                split_ready(v, None)
                for t in range(NT):
                    for k in range(KD):
                        last = products(dst[:, t, :], tuple(m[:, k, t * P:(t + 1) * P] for m in xs), w_cols(v, k),
                                        k == 0, k == KD - 1)
                last.then_inc(sem["half_done"], 1)

            def take():
                v_next[0] += 1
                return v_next[0] - 1

            def col_unit(b, xs, first=False):
                for f in range(2):
                    transposed(take(), bank[:, b, f * T:(f + 1) * T], xs, first=first and f == 0)

            def nat_unit(b, xs):
                v = take()
                split_ready(take(), None)
                slot = v % SPL
                for t in range(NT):
                    for k in range(KD):
                        last = products(bank[:, b, t * UC:(t + 1) * UC], tuple(m[:, k, t * P:(t + 1) * P] for m in xs),
                                        tuple(m[:, slot:slot + 2, k * P:(k + 1) * P] for m in (w_hi, w_lo)),
                                        k == 0, k == KD - 1)
                last.then_inc(sem["half_done"], 2)

            def row_half(v, out_of, ys, tile, start, stop, i=None):
                split_ready(v, i)
                for t in range(NT):
                    for n in range(2):
                        last = products(out_of(t, n), tuple(m[:, tile, t * P:(t + 1) * P] for m in ys),
                                        w_cols(v, n, 512), start, stop)
                last.then_inc(sem["half_done"], 1)

            def last_rows(v, ys, tile):
                split_ready(v + 1, None)
                for t in range(NT):
                    for n in range(2):
                        for s in range(2):
                            last = products(d_bank(t, n), tuple(m[:, tile + s, t * P:(t + 1) * P] for m in ys),
                                            w_cols(v + s, n, 512), False, s == 1)
                            if t == 1 and n == 1:
                                last.then_inc(sem["half_done"], 1)
                        if not (t == 1 and n == 1):
                            last.then_inc(sem["acc_ready"], 1)

            def row_units(n_tiles, ys):
                for tile in range(n_tiles - 2):
                    row_half(take(), d_bank, ys, tile, tile == 0, False)
                last_rows(take(), ys, n_tiles - 2)
                take()

            def norm(loaded=False):
                for t, ks in ((0, range(4)), (0, (4, 5)), (0, (6,)), (1, range(4)), (0, (7,)), (1, range(4, 8))):
                    if not loaded and ks[0] in (0, 4, 6, 7) and (t, ks[0]) not in ((1, 0), (1, 4)):
                        c.next("residual")
                    for k in ks:
                        last = pe.transpose(bank[:, k, t * P:(t + 1) * P], x[:, t, k * P:(k + 1) * P], ident[:, :])
                        if t == 1:
                            last.then_inc(sem["xT_psum"], 1)

            def scale_broadcast(b):
                c.next("diag_ready")
                pe.matmul(bank[:, b, 0:T], unit_sq[:, :], diag[:, :, :].rearrange("p t i -> p (t i)"), start=True,
                          stop=True).then_inc(sem["scale_psum"], 1)

            n_ffn = [0]

            def ffn(late=False, first_up=None):
                v0, j0 = 2 * ffns[n_ffn[0]][0], NJ * n_ffn[0]
                n_ffn[0] += 1
                assert v_next[0] == v0

                def gate_up(j, i=None):
                    v = v0 + (4 + 6 * (j - 1) if j else 0)
                    for n in range(4):
                        if (j == 0 and n == 3 and not late) or (j == 1 and n == 1 and late):
                            scale_broadcast(4)
                        dst = bank[:, 2 * (j % 2) + n // 2, (n % 2) * T:(n % 2 + 1) * T]
                        transposed(v + n, dst, X, i, first=j == 0 and n == 0)

                def down(j, v, i=None):
                    ready = j0 + j + 1
                    pe.wait_ge(sem["hidden_lo_ready"], ready if i is None else ready + 2 * i)
                    if j == NJ - 1:
                        last_rows(v, HID, 2 * (j % 2))
                        return
                    for s in range(2):
                        row_half(v + s, d_bank, HID, 2 * (j % 2) + s, j == 0 and s == 0, False, i)

                gate_up(0)
                if first_up is not None:
                    first_up()
                gate_up(1)
                if n_ffn[0] == 1:
                    memory_and_vectors()
                    relative_bias()
                if first_up is not None:
                    c.next("y_lo_ready")
                down(0, v0 + 8)
                with pe.Fori(0, LOOPS) as i:
                    for j in (2, 3):
                        gate_up(j, i)
                        down(j - 1, v0 + 6 * j + 2, i)
                gate_up(NJ - 1)
                down(NJ - 2, v0 + 6 * (NJ - 1) + 2)
                down(NJ - 1, v0 + FFN_HALVES - 2)
                v_next[0] = v0 + FFN_HALVES

            def score_groups(groups, q_of, k_of):
                for g, (t, heads, nk) in enumerate(groups):
                    for n, h in enumerate(heads):
                        last = pe.matmul(bank[:, g, n * nk:(n + 1) * nk], q_of(h, t), k_of(h, nk), start=True, stop=True)
                    last.then_inc(sem["scores"], 1)

            def transpose_probs(groups):
                for g, (t, heads, nk) in enumerate(groups):
                    c.next("probs_ready")
                    for blk in range(4):
                        last = pe.transpose(bank[:, (len(groups) + g) % 8, blk * P:(blk + 1) * P],
                                            prob[:, g, blk * P:(blk + 1) * P], ident[:, :])
                    last.then_inc(sem["probT_psum"], 1)

            def values(groups, v_of, out_of, last_head):
                for g, (t, heads, nk) in enumerate(groups):
                    c.next("probT_odd" if g % 2 else "probT_even")
                    for n, h in enumerate(heads):
                        for kb in range(nk // P):
                            blk = n * (nk // P) + kb
                            last = pe.matmul(out_of(h, t), v_of(h, kb), probT[:, g, blk * P:(blk + 1) * P],
                                             start=kb == 0, stop=kb == nk // P - 1)
                        if h in last_head:
                            last.then_inc(sem["out_psum"], 1)

            def memory_and_vectors():
                pe.wait_ge(sem["vectors_loaded"], 16 * (len(VECTORS) - 1))
                n = N_COLS - P
                pe.wait_ge(sem["gain_loaded"], 16)
                for k in range(KD):
                    pe.transpose(bank[:, 7, T + k:T + k + 1], gain_row[0:1, k * P:(k + 1) * P], ident[0:1, 0:1])
                pe.transpose(bank[:, 7, 0:P], col_rows[:, 0, :], ident[:, :])
                pe.transpose(bank[:, 7, P:N_COLS], col_rows[0:n, 1, :], ident[0:n, 0:n]).then_inc(sem["vectors_psum"], 1)
                c.next("mem_normed", 2)
                c.next("cols_ready")
                pe.wait_ge(sem["scale_ready"], 1)
                for k in range(KD):
                    for t in range(NT):
                        at = (k % 2) * T + t * P
                        last = pe.transpose(bank[:, 4 + k // 2, at:at + P], mem_in[:, t, k * P:(k + 1) * P], ident[:, :])
                    if k % 2:
                        last.then_inc(sem["xT_psum"], 1)

            def transpose_p():
                pe.wait_ge(sem["p_loaded"], 16)
                for k in range(2):
                    for t in range(NT):
                        last = pe.transpose(bank[:, 5, k * T + t * P:k * T + (t + 1) * P],
                                            p_in[:, t, k * P:(k + 1) * P], ident[:, :])
                last.then_inc(sem["out_psum"], 1)

            def relative_bias():
                c.next("xT_lo_ready", 4)
                pe.wait_ge(sem["bias_rev_loaded"], 16)
                for n in range(4):
                    pe.matmul(bank[:, 4 + n, :], flip, bias_rev[:, 2 * n:2 * n + 2, :], start=True, stop=True)\
                        .then_inc(sem["bias_psum"], 1)
                c.next("bias_ready", 4)

            pe.wait_ge(sem["pool_const"], 6)
            pe.wait_ge(sem["first_gains_loaded"], 16)
            pe.transpose(bank[:, 7, 256:272], col_rows[0:16, 0, :], ident[0:16, 0:16]).then_inc(sem["first_gains_psum"], 1)
            c.next("cols_ready")
            pe.wait_ge(sem["x_loaded"], 16)
            norm(loaded=True)
            ffn()
            norm()
            col_unit(0, X, first=True)
            col_unit(1, X)
            v = take()
            transposed(v, bank[:, 2, 0:T], X)
            scale_broadcast(5)
            natural(take(), bank[:, 3, 0:T].rearrange("p (t f) -> p t f", t=NT), X)
            col_unit(6, X)
            col_unit(7, X)
            c.next("proj_sb", 3)
            c.next("nat_sb", 1)
            score_groups(SWA_GROUPS,
                         lambda h, t: q_sb[64 * (h // 4):64 * (h // 4) + 64, h % 4, t * P:(t + 1) * P],
                         lambda h, nk: swa_k[64 * (h // 4):64 * (h // 4) + 64, 0:nk])
            for b in (6, 7, 6, 7):
                c.next("nat_sb")
                col_unit(b, X)
            c.next("nat_sb", 2)
            transpose_probs(SWA_GROUPS)
            values(SWA_GROUPS, lambda h, kb: swa_v[:, kb, 64 * (h // 4):64 * (h // 4) + 64],
                   lambda h, t: bank[64 * (h % 2):64 * (h % 2) + 64, 4 + t, (h // 2) * P:(h // 2 + 1) * P], (7,))
            c.next("y_lo_ready", 2)
            for tile in (4, 5, 6, 7):
                row_half(take(), d_bank, Y, tile, tile == 4, False)
            c.next("y_lo_ready", 2)
            for tile in (0, 1):
                row_half(take(), d_bank, Y, tile, False, False)
            last_rows(take(), Y, 2)
            take()

            def cross(kv):
                norm()
                col_unit(0, X, first=True)
                transposed(take(), bank[:, 1, 0:T], X)
                scale_broadcast(7)
                transposed(take(), bank[:, 1, T:2 * T], X)
                if kv:
                    for b in (4, 5):
                        col_unit(b, MEM)
                    c.next("nat_sb", 2)
                c.next("proj_sb", 2)
                score_groups(XA_GROUPS, lambda h, t: q_sb[:, h, t * P:(t + 1) * P], lambda h, nk: mem_k[:, h, :])
                if kv:
                    for b in (6, 7):
                        nat_unit(b, MEM)
                    c.next("nat_sb", 2)
                transpose_probs(XA_GROUPS)
                values(XA_GROUPS, lambda h, kb: mem_v[:, kb, h * P:(h + 1) * P],
                       lambda h, t: bank[:, t, h * P:(h + 1) * P], (3,))
                c.next("y_lo_ready", 2)
                row_units(4, Y)

            cross(True)
            norm()
            ffn()
            norm()
            ffn()
            norm()
            for b in range(6):
                col_unit(b, X, first=b == 0)
                if b == 1:
                    scale_broadcast(7)
            for b in (6, 7):
                nat_unit(b, X)
            c.next("proj_sb", 6)
            c.next("nat_sb", 2)
            score_groups(MOBA_GROUPS, lambda h, t: q_sb[:, h, t * P:(t + 1) * P], lambda h, nk: k_sb[:, h // 2, 0:nk])
            for n, b in enumerate((6, 7, 6, 7)):
                if n >= 2:
                    c.next("nat_sb")
                (col_unit if n < 2 else nat_unit)(b, MEM)
            c.next("nat_sb", 2)
            transpose_probs(MOBA_GROUPS)
            values(MOBA_GROUPS, lambda h, kb: v_sb[:, kb, (h // 2) * P:(h // 2 + 1) * P],
                   lambda h, t: bank[:, 4 + 2 * t + h // 4, (h % 4) * P:(h % 4 + 1) * P], (3, 7))
            c.next("y_lo_ready", 4)
            row_units(8, Y)
            cross(False)
            norm()
            ffn()
            norm()
            c.skip("residual", 4)
            ffn(late=True)
            norm()
            for half in range(2):
                v = take()
                split_ready(v, None)
                for k in range(4 * half, 4 * half + 4):
                    c.next("xT_lo_ready")
                    last = products(bank[:, 0, 0:T], w_cols(v, k % 4), xk(X, k), k == 0, k == KD - 1)
                last.then_inc(sem["half_done"], 1)
            transposed(take(), bank[:, 5, 0:T], X)
            scale_broadcast(7)
            transposed(take(), bank[:, 5, T:2 * T], X)
            c.next("proj_sb")
            pe.wait_ge(sem["rank_loaded"], 16)
            for i in range(2):
                last = pe.matmul(bank[:, 7, i * T:(i + 1) * T], rank_w[:, i * P:(i + 1) * P], rank_x[:, :],
                                 start=True, stop=True)
            last.then_inc(sem["rank_psum"], 1)
            col_unit(6, X)
            for b in (1, 2, 3, 4):
                col_unit(b, X)
            c.next("decays")
            nat_unit(7, X)
            nat_unit(0, X)
            c.next("proj_sb", 4)
            c.next("nat_sb", 4)
            nat_unit(1, X)
            nat_unit(2, X)
            c.next("nat_sb", 4)

            def tile_at(m, i, tt, h):
                return m[64 * h:64 * h + 64, i * T + tt * P:i * T + (tt + 1) * P]

            for b, (k, q) in ((0, (k_neg, q_dec)), (2, (k_pos, q_neg))):
                c.next("gla_operands")
                for h in range(2):
                    for tt in range(NT):
                        for i in range(2):
                            at = (2 * tt + i) * P
                            last = pe.matmul(bank[:, b + h, at:at + P], tile_at(k, i, tt, h), tile_at(q, i, tt, h),
                                             start=True, stop=True)
                last.then_inc(sem["gla_scores"], 1)
            c.next("gla_operands")
            for tt in range(NT):
                for i in range(2):
                    last = pe.transpose(bank[:, 4, (2 * tt + i) * P:(2 * tt + i + 1) * P],
                                        k_end[:, i * T + tt * P:i * T + (tt + 1) * P], ident[:, :])
            last.then_inc(sem["k_nat_psum"], 1)
            c.next("k_nat_ready")
            for ch in (0, 2, 1):
                tt, r = ch // 2, ch % 2
                for h in range(2):
                    for i in range(2):
                        head = 2 * i + h
                        at = (2 * tt + i) * P if r == 0 else i * P
                        last = pe.matmul(bank[64 * h:64 * h + 64, 6 + r, at:at + P],
                                         k_nat[64 * r:64 * r + 64, (2 * tt + i) * P + 64 * h:(2 * tt + i) * P + 64 * h + 64],
                                         g_v[64 * r:64 * r + 64, tt, head * P:(head + 1) * P], start=True, stop=True)
            last.then_inc(sem["kv_psum"], 1)

            def conv_tile(tile, b):
                for j in range(CONV_TAPS):
                    last = pe.matmul(bank[:, b, 0:T], tap_diag(tile, j), glu[:, tile, j:j + T],
                                     start=j == 0, stop=j == CONV_TAPS - 1)
                last.then_inc(sem["conv_psum"], 1)

            pe.wait_ge(sem["glu_ready"], 2)
            pe.wait_ge(sem["tap_diags"], 2 * CONV_TAPS)
            conv_tile(2, 5)
            c.next("score_ready", 4)
            c.next("states_ready")
            for h in range(2):
                for tt in range(NT):
                    for i in range(2):
                        head, at = 2 * i + h, (2 * tt + i) * P
                        pe.matmul(bank[:, h, at:at + P], score[:, h, at:at + P], g_v[:, tt, head * P:(head + 1) * P],
                                  start=True, stop=False, skip_group_check=True)
                        for ch in (1,) if tt == 0 else (2, 3):
                            r = ch % 2
                            last = pe.matmul(bank[64 * r:64 * r + 64, h, at:at + P],
                                             q_dec[64 * h:64 * h + 64, i * T + ch * 64:i * T + ch * 64 + 64],
                                             state[64 * h:64 * h + 64, ch - 1, i * P:(i + 1) * P],
                                             start=False, stop=True, skip_group_check=True)
            last.then_inc(sem["out_psum"], 1)
            conv_tile(3, 6)
            c.next("gated", 2)
            for head in range(4):
                for tt in range(NT):
                    at = (head % 2) * T + tt * P
                    last = pe.transpose(bank[:, 2 + head // 2, at:at + P], o_nat[:, tt, head * P:(head + 1) * P],
                                        ident[:, :])
                if head % 2:
                    last.then_inc(sem["out_psum"], 1)
            c.next("conv_evac", 2)
            pe.wait_ge(sem["conv_tap"], DVE_TILES * CONV_TAPS)
            for n in range(4):
                last = pe.matmul(bank[:, 0, 0:T], ones, conv_acc[:, n, :], start=n == 0, stop=n == 3)
            last.then_inc(sem["mean_psum"], 1)
            c.next("y_lo_ready", 2)
            row_half(take(), d_bank, Y, 4, True, False)
            c.next("var_in", 2)
            for n in range(4):
                last = pe.matmul(bank[:, 1, 0:T], ones, sq_c[:, n, :], start=n == 0, stop=n == 3)
            last.then_inc(sem["var_psum"], 1)
            for tile in (5, 6, 7):
                row_half(take(), d_bank, Y, tile, False, False)
            c.next("y_lo_ready")
            for tile in (0, 1):
                row_half(take(), d_bank, Y, tile, False, False)
            c.next("y_lo_ready")
            last_rows(take(), Y, 2)
            take()
            norm()
            ffn(first_up=transpose_p)
            norm()
            c.next("xT_lo_ready", 4)
            for tile in range(2):
                row_half(take(), lambda t, n: bank[:, 2 * t + n, :], Y, tile, tile == 0, tile == 1)
            c.next("xT_lo_ready", 4)
            row_units(KD, X)
            assert v_next[0] == n_half


def kernel(**inputs):
    import concourse.bacc as bacc
    from concourse.bass_utils import run_bass_kernel_spmd

    nc = bacc.Bacc("TRN2", target_bir_lowering=False, num_devices=1)
    arrays, aps = {}, {}
    for name, value in inputs.items():
        array = np.ascontiguousarray(value)
        arrays[f"in_{name}"] = array
        aps[name] = nc.dram_tensor(f"in_{name}", array.shape, mybir.dt.from_np(array.dtype), kind="ExternalInput").ap()
    out = nc.dram_tensor("result", (1, T, D), F32, kind="ExternalOutput").ap()
    build(nc, aps, out)
    r = run_bass_kernel_spmd(nc, [arrays], core_ids=[0])
    return r.results[0]["result"]
```
